# Optimizing a Trainium2 kernel written in Bass

```python
import math
import jax, jax.numpy as jnp
from jax import lax
import numpy as np

D_MODEL = 1024
BATCH = 1
SEQ = 1024
DEPTH = 1

ATT_HEADS = 16
ATT_KV_HEADS = 4
ATT_HEAD_DIM = D_MODEL // ATT_HEADS
ATT_WIDTH = ATT_HEADS * ATT_HEAD_DIM
ATT_KV_WIDTH = ATT_KV_HEADS * ATT_HEAD_DIM
WINDOW = 128
BLOCK = WINDOW
ROPE_THETA = 10000.0
M_HEADS = 4
M_HEAD_DIM = D_MODEL // M_HEADS
M_WIDTH = M_HEADS * M_HEAD_DIM
M_CHUNK = 64
CONV_WIDTH = 4
EPS = 1e-6
POS_OFFSET_MAX = 1024
IN_SPLITS = (ATT_WIDTH, ATT_KV_WIDTH, ATT_KV_WIDTH, ATT_WIDTH,
             M_WIDTH, M_WIDTH, M_WIDTH, M_WIDTH, M_WIDTH,
             M_HEADS, M_HEADS,
             D_MODEL, D_MODEL)
IN_WIDTH = sum(IN_SPLITS)

kernel_name = 'hybrid_swa_sink_mlstm_gated_adaln'

def rmsnorm(x, w):
    x32 = x.astype(jnp.float32)
    y = x32 * lax.rsqrt(jnp.mean(x32 * x32, axis=-1, keepdims=True) + EPS)
    return (y * w.astype(jnp.float32)).astype(x.dtype)

def rope(x, positions):
    hd = x.shape[-1]
    inv_freq = ROPE_THETA ** (-jnp.arange(0, hd, 2, dtype=jnp.float32) / hd)
    ang = positions.astype(jnp.float32)[..., None] * inv_freq
    cos = jnp.cos(ang)[:, :, None, :]
    sin = jnp.sin(ang)[:, :, None, :]
    x32 = x.astype(jnp.float32)
    x1, x2 = jnp.split(x32, 2, axis=-1)
    out = jnp.concatenate([x1 * cos - x2 * sin, x2 * cos + x1 * sin], axis=-1)
    return out.astype(x.dtype)

def sliding_window_attention(q, k, v, sinks):
    B, S, Hq, hd = q.shape
    Hkv = k.shape[2]
    G = Hq // Hkv
    NB = S // BLOCK
    qb = q.reshape(B, NB, BLOCK, Hkv, G, hd)
    kb = k.reshape(B, NB, BLOCK, Hkv, hd)
    vb = v.reshape(B, NB, BLOCK, Hkv, hd)
    pad = ((0, 0), (1, 0), (0, 0), (0, 0), (0, 0))
    kk = jnp.concatenate([jnp.pad(kb, pad)[:, :-1], kb], axis=2)
    vv = jnp.concatenate([jnp.pad(vb, pad)[:, :-1], vb], axis=2)
    scores = jnp.einsum('bnqhgd,bnkhd->bnhgqk', qb, kk).astype(jnp.float32) * (hd ** -0.5)
    q_in = BLOCK + jnp.arange(BLOCK)
    k_in = jnp.arange(2 * BLOCK)
    rel = q_in[:, None] - k_in[None, :]
    band = (rel >= 0) & (rel < WINDOW)
    key_abs = jnp.arange(NB)[:, None] * BLOCK - BLOCK + k_in[None, :]
    mask = band[None] & (key_abs >= 0)[:, None, :]
    scores = jnp.where(mask[None, :, None, None], scores, -jnp.inf)
    sink = sinks.astype(jnp.float32).reshape(1, 1, Hkv, G, 1, 1)
    mx = jnp.maximum(scores.max(axis=-1, keepdims=True), sink)
    p = jnp.exp(scores - mx)
    probs = p / (p.sum(axis=-1, keepdims=True) + jnp.exp(sink - mx))
    out = jnp.einsum('bnhgqk,bnkhd->bnqhgd', probs.astype(v.dtype), vv)
    return out.reshape(B, S, Hq * hd)

def causal_conv(x, w):
    S = x.shape[1]
    xp = jnp.pad(x, ((0, 0), (CONV_WIDTH - 1, 0), (0, 0)))
    return sum(w[j] * xp[:, j:j + S] for j in range(CONV_WIDTH))

def mlstm_chunkwise(q, k, v, i_pre, logf):
    B, S, H, d = q.shape
    L = M_CHUNK
    NC = S // L
    def chunks(t):
        return t.astype(jnp.float32).reshape(B, NC, L, H, d).transpose(1, 0, 3, 2, 4)
    def gchunks(t):
        return t.astype(jnp.float32).reshape(B, NC, L, H).transpose(1, 0, 3, 2)
    causal = jnp.tril(jnp.ones((L, L), dtype=bool))

    def step(carry, inp):
        C, n, m = carry
        qc, kc, vc, ic, fc = inp
        b = jnp.cumsum(fc, axis=-1)
        log_d = jnp.where(causal, b[..., :, None] - b[..., None, :] + ic[..., None, :], -jnp.inf)
        log_inter = b + m[..., None]
        m_t = jnp.maximum(log_inter, log_d.max(axis=-1))
        w_inter = jnp.exp(log_inter - m_t)
        s = jnp.einsum('bhtd,bhsd->bhts', qc, kc) * jnp.exp(log_d - m_t[..., None])
        num = w_inter[..., None] * jnp.einsum('bhtk,bhkv->bhtv', qc, C) + jnp.einsum('bhts,bhsv->bhtv', s, vc)
        nq = w_inter * jnp.einsum('bhtk,bhk->bht', qc, n) + s.sum(axis=-1)
        h = num / jnp.maximum(jnp.abs(nq), jnp.exp(-m_t))[..., None]
        b_last = b[..., -1]
        log_w = b_last[..., None] - b + ic
        m_new = jnp.maximum(b_last + m, log_w.max(axis=-1))
        decay = jnp.exp(b_last + m - m_new)
        w = jnp.exp(log_w - m_new[..., None])
        C_new = decay[..., None, None] * C + jnp.einsum('bhs,bhsk,bhsv->bhkv', w, kc, vc)
        n_new = decay[..., None] * n + jnp.einsum('bhs,bhsk->bhk', w, kc)
        return (C_new, n_new, m_new), h

    init = (jnp.zeros((B, H, d, d), jnp.float32), jnp.zeros((B, H, d), jnp.float32), jnp.zeros((B, H), jnp.float32))
    _, hs = lax.scan(step, init, (chunks(q), chunks(k), chunks(v), gchunks(i_pre), gchunks(logf)))
    return hs.transpose(1, 0, 3, 2, 4).reshape(B, S, H, d)

def setup_inputs(seed: int = 0) -> dict:
    key = jax.random.key(seed)
    ks = jax.random.split(key, 20)
    D = D_MODEL
    nrm = lambda k, shape, fan_in: jax.random.normal(k, shape, jnp.float32) * (fan_in ** -0.5)
    x = jax.random.normal(ks[0], (BATCH, SEQ, D), jnp.float32)
    c = jax.random.normal(ks[1], (BATCH, D), jnp.float32)
    offset = jax.random.randint(ks[2], (BATCH, 1), 0, POS_OFFSET_MAX, dtype=jnp.int32)
    positions = (offset + jnp.arange(SEQ, dtype=jnp.int32)[None, :]).astype(jnp.int32)
    w_ada = nrm(ks[3], (DEPTH, D, 3 * D), D)
    b_ada = 0.01 * jax.random.normal(ks[4], (DEPTH, 3 * D), jnp.float32)
    norm_w = 1.0 + 0.02 * jax.random.normal(ks[5], (DEPTH, D), jnp.float32)
    w_in = nrm(ks[6], (DEPTH, D, IN_WIDTH), D)
    b_i = 0.1 * jax.random.normal(ks[7], (DEPTH, M_HEADS), jnp.float32)
    b_f = jnp.linspace(3.0, 6.0, M_HEADS, dtype=jnp.float32)[None, :] + 0.1 * jax.random.normal(ks[8], (DEPTH, M_HEADS), jnp.float32)
    b_if = jnp.concatenate([b_i, b_f], axis=-1)
    att_sinks = 0.5 * jax.random.normal(ks[9], (DEPTH, ATT_HEADS), jnp.float32)
    conv_q = nrm(ks[10], (DEPTH, CONV_WIDTH, M_WIDTH), CONV_WIDTH)
    conv_k = nrm(ks[11], (DEPTH, CONV_WIDTH, M_WIDTH), CONV_WIDTH)
    m_norm_w = 1.0 + 0.02 * jax.random.normal(ks[12], (DEPTH, M_WIDTH), jnp.float32)
    w_att_branch = nrm(ks[13], (DEPTH, ATT_WIDTH, D), ATT_WIDTH)
    w_m_branch = nrm(ks[14], (DEPTH, M_WIDTH, D), M_WIDTH)
    w_out = nrm(ks[15], (DEPTH, D, D), D)
    final_norm_w = 1.0 + 0.02 * jax.random.normal(ks[16], (D,), jnp.float32)
    return {'x': x, 'c': c, 'positions': positions, 'w_ada': w_ada, 'b_ada': b_ada, 'norm_w': norm_w,
            'w_in': w_in, 'b_if': b_if, 'att_sinks': att_sinks, 'conv_q': conv_q, 'conv_k': conv_k,
            'm_norm_w': m_norm_w, 'w_att_branch': w_att_branch, 'w_m_branch': w_m_branch,
            'w_out': w_out, 'final_norm_w': final_norm_w}

def reference(x, c, positions, w_ada, b_ada, norm_w, w_in, b_if, att_sinks, conv_q, conv_k,
              m_norm_w, w_att_branch, w_m_branch, w_out, final_norm_w):
    B, S, _ = x.shape
    split_idx = np.cumsum(IN_SPLITS)[:-1].tolist()
    for l in range(DEPTH):
        mod = jax.nn.silu(c) @ w_ada[l] + b_ada[l]
        shift, scale, gate = jnp.split(mod, 3, axis=-1)
        h = rmsnorm(x, norm_w[l]) * (1.0 + scale[:, None, :]) + shift[:, None, :]
        proj = h @ w_in[l]
        aq, ak, av, az, mq, mk, mv, mo, mz, mi, mf, ga, gm = jnp.split(proj, split_idx, axis=-1)
        aq = rope(aq.reshape(B, S, ATT_HEADS, ATT_HEAD_DIM), positions)
        ak = rope(ak.reshape(B, S, ATT_KV_HEADS, ATT_HEAD_DIM), positions)
        av = av.reshape(B, S, ATT_KV_HEADS, ATT_HEAD_DIM)
        att = sliding_window_attention(aq, ak, av, att_sinks[l])
        y_att = (att * jax.nn.silu(az)) @ w_att_branch[l]
        mq = jax.nn.silu(causal_conv(mq, conv_q[l])).reshape(B, S, M_HEADS, M_HEAD_DIM)
        mk = (jax.nn.silu(causal_conv(mk, conv_k[l])) * (M_HEAD_DIM ** -0.5)).reshape(B, S, M_HEADS, M_HEAD_DIM)
        mv = mv.reshape(B, S, M_HEADS, M_HEAD_DIM)
        b_i, b_f = jnp.split(b_if[l], 2)
        i_pre = (mi + b_i).astype(jnp.float32)
        logf = jax.nn.log_sigmoid((mf + b_f).astype(jnp.float32))
        hm = mlstm_chunkwise(mq, mk, mv, i_pre, logf)
        hm = hm * lax.rsqrt(jnp.mean(hm * hm, axis=-1, keepdims=True) + EPS)
        hm = (hm.reshape(B, S, M_WIDTH) * m_norm_w[l].astype(jnp.float32)).astype(x.dtype)
        hm = hm * jax.nn.sigmoid(mo)
        y_m = (hm * jax.nn.silu(mz)) @ w_m_branch[l]
        merged = jax.nn.sigmoid(ga) * y_att + jax.nn.sigmoid(gm) * y_m
        x = x + gate[:, None, :] * (merged @ w_out[l])
    return rmsnorm(x, final_norm_w)


_drawn_inputs = setup_inputs


def setup_inputs(seed=0):
    import zlib

    import numpy as np

    out = dict(_drawn_inputs(seed))
    spreads = {}
    factors = {'b_ada': 8.0,
     'norm_w': 7.333,
     'att_sinks': 200.0,
     'conv_q': 2.944,
     'conv_k': 2.836,
     'm_norm_w': 130.304,
     'final_norm_w': 24.875}
    for name, (base, spread) in spreads.items():
        noise = np.random.default_rng([zlib.crc32(name.encode()), seed]).standard_normal(out[name].shape)
        drawn = base * np.exp(spread * noise) if base else spread * noise
        out[name] = __import__('jax').numpy.asarray(drawn.astype(out[name].dtype))
    for name, factor in factors.items():
        out[name] = (out[name] * factor).astype(out[name].dtype)
    return out
```

```python
from contextlib import ExitStack

import numpy as np

import concourse.bass as bass
from concourse import mybir

F32 = mybir.dt.float32
F32R = mybir.dt.float32r
BF16 = mybir.dt.bfloat16
I32 = mybir.dt.int32
ALU = mybir.AluOpType
ACT = mybir.ActivationFunctionType
AX = mybir.AxisListType

P = 128
D = 1024
S = 1024
KT = D // P
NB = S // P
HALF = 512
HD = 64
KVH = 4
MH = 4
MD = 256
MV = MD + 1
CW = 4
EPS = 1e-6
NEG = -1e30
ATT_SCALE = HD ** -0.5
K_SCALE = MD ** -0.5
(AQ, AK, AV, AZ, MQ, MK, MVC, MO, MZ, MI, MF, GA, GM) = np.cumsum(
    [0, 1024, 256, 256, 1024, 1024, 1024, 1024, 1024, 1024, 4, 4, 1024]).tolist()
V_C, V_NW, V_SH, V_SC, V_CQ, V_CK, V_MN, V_N = 0, 8, 16, 24, 32, 64, 96, 104
TWO_PI = 6.283185307179586
PI_A = 6.25
PI_B = 0.033203125
PI_C = TWO_PI - PI_A - PI_B
PI_C1 = float(np.float32(round(PI_C * 2 ** 24) / 2 ** 24))
PI_C2 = PI_C - PI_C1
PI_TOP = 3.1415925

SLOT_USES = {"G": (1, 0, 0, 0, 0), "A": (4,) * 5, "B": (4, 4, 4, 4, 0), "C": (8,) * 5,
             "D1": (2, 2, 2, 2, 0), "D2": (2, 2, 2, 2, 0), "E": (1, 1, 1, 1, 0), "E2": (1, 1, 1, 1, 0)}
SLOT_DMAS = {"G": (2, 0, 0, 0, 0), "A": (4, 4, 8, 4, 4), "B": (4, 4, 4, 4, 0), "C": (8,) * 5,
             "D1": (2, 2, 2, 2, 0), "D2": (2, 2, 2, 2, 0), "E": (1, 1, 1, 1, 0), "E2": (1, 1, 1, 1, 0)}
BANK_USES = {"G": 1, "A": 24, "B": 16, "C": 48, "D1": 8, "D2": 8, "E": 8}


def before(table, phase, slot=None):
    total = 0
    for name, n in table.items():
        if name == phase:
            return total
        total += n if slot is None else n[slot]


C_UNITS = [("mq", 0), ("mq", 1), ("mq", 2), ("mq", 3), ("mk", 0), ("mk", 1), ("mk", 2), ("mk", 3)]
for _u in range(NB):
    C_UNITS.append(("mv", _u))
    if _u % 2 == 0:
        C_UNITS.append(("mz", _u // 2))
C_UNITS += [("mo", 0), ("mo", 1), ("mo", 2), ("mo", 3)]
C_LOADS = [(MQ, 0, 0), (MQ + P, 1, 0), (MK, 2, 0), (MK + P, 3, 0), (MZ, 4, 0),
           (MVC, 0, 1), (MVC + P, 1, 1), (MZ + P, 2, 1), (MO, 3, 1), (MO + P, 4, 1)]
C_MASK_AFTER = 2


def build(nc, x, c, positions, w_ada, b_ada, norm_w, w_in, b_if, att_sinks, conv_q, conv_k,
          m_norm_w, w_att, w_m, w_out, final_norm_w, inv_freq, out, row_pack, merged_dram):
    with ExitStack() as ctx:
        counters = []

        def sb(name, shape, dt=F32):
            return ctx.enter_context(nc.sbuf_tensor(name, shape, dt))

        def sem(name):
            return ctx.enter_context(nc.semaphore(name))

        def counter(name, start=1):
            s = sem(name)
            counters.append((s, start))
            return s

        def after(eng, s, n):
            eng.wait_ge(s, n + 1)

        ident = sb("ident", [P, P])
        ident_bf = sb("ident_bf", [P, P], BF16)
        ones = sb("ones", [P, P])
        causal = sb("causal", [P, P])
        vec_rows = sb("vec_rows", [V_N, P])
        vecs = sb("vecs", [P, V_N])
        silu_c = sb("silu_c", [P, KT])
        pos_i = sb("pos_i", [NB, P], I32)
        pos_f = sb("pos_f", [NB, P])
        pos_col = sb("pos_col", [P, NB])
        freq = sb("freq", [P, HD // 2])
        sink = sb("sink", [P, 16])
        neg_sink = sb("neg_sink", [P, 16])
        bias_if = sb("bias_if", [36, 1])
        scale1 = sb("scale1", [P, KT])
        scale_t = sb("scale_t", [P, KT])
        shift = sb("shift", [P, KT])
        x_ssq = sb("x_ssq", [P, NB])
        x_rstd = sb("x_rstd", [P, NB])
        neg_half = sb("neg_half", [P, NB])
        m_prev = sb("m_prev", [4, NB])
        cols = sb("cols", [P, MH, NB, 4])
        h_cols = sb("h_cols", [P, NB, 4])
        taps_q = sb("taps_q", [P, CW, 2])
        taps_k = sb("taps_k", [P, CW, 2])
        m_norm = sb("m_norm", [P, 2])
        h_neg_sink = sb("h_neg_sink", [P, 2, 2])
        s_max = sb("s_max", [P, 4])
        neg_m = sb("neg_m", [P, 4])
        sink_d = sb("sink_d", [P, 4])
        p_sum = sb("p_sum", [P, 4])
        sink_e = sb("sink_e", [P, 4])
        p_den = sb("p_den", [P, 4])
        p_rec = sb("p_rec", [P, 4])
        h_den = sb("h_den", [P, NB])
        h_rec = sb("h_rec", [P, NB])
        h_ssq = sb("h_ssq", [P, NB])
        h_ms = sb("h_ms", [P, NB])
        h_rms = sb("h_rms", [P, NB])
        h_inv = sb("h_inv", [P, NB])
        h_scale = sb("h_scale", [P, NB])
        o_ssq = sb("o_ssq", [P, NB, 2])
        o_sum = sb("o_sum", [P, NB])
        o_ms = sb("o_ms", [P, NB])
        o_rms = sb("o_rms", [P, NB])
        o_rstd = sb("o_rstd", [P, NB])

        base = (nc.sbuf_base + 63) // 64 * 64
        at = {}

        def place(name, shape, dt, offset):
            at[name] = offset
            return nc.alloc_sbuf_tensor_at(name, shape, dt, offset=base + offset)

        K32 = KT * S * 4
        HT, RAW = 0, 2 * K32
        WHI, WLO = RAW + 5 * 4096, RAW + 10 * 4096
        YO = WLO + 5 * 4096
        SCR = YO + K32
        X = SCR + K32
        h_hi = place("h_hi", [P, KT, S], F32R, HT)
        h_lo = place("h_lo", [P, KT, S], F32R, HT + K32)
        raw = place("raw", [P, 5, KT, P], F32, RAW)
        w_hi = place("w_hi", [P, 5, KT, P], F32R, WHI)
        w_lo = place("w_lo", [P, 5, KT, P], F32R, WLO)
        y = place("y", [P, KT, S], F32, YO)
        y_lo = place("y_lo", [P, KT, S], F32R, YO)
        w_mod = place("w_mod", [P, KT, 2 * D], F32, HT)
        x_in = place("x_in", [P, NB, D], F32, YO)
        xnt = place("xnt", [P, KT, S], F32, SCR)
        cos = place("cos", [P, NB, HD // 2], F32, X)
        sin = place("sin", [P, NB, HD // 2], F32, X + 1024)
        band = place("band", [P, 2 * P], BF16, X + 2048)
        band0 = place("band0", [P, 2 * P], BF16, X + 2560)
        mod_acc = place("mod_acc", [P, 2 * D], F32, X + 3072)
        ang = place("ang", [P, NB, HD // 2], F32, X + 11264)
        turns = place("turns", [P, NB, HD // 2], F32, X + 12288)
        turns_i = place("turns_i", [P, NB, HD // 2], I32, X + 13312)
        row_if = place("row_if", [P, S], F32, YO)
        row_e = place("row_e", [P, S], F32, YO + 4096)
        row_logf = place("row_logf", [P, S], F32, YO + 8192)
        row_b = place("row_b", [P, S], F32, YO + 12288)
        row_m = place("row_m", [P, S], F32, YO + 16384)
        row_c = place("row_c", [P, S], F32, YO + 20480)
        row_keep = place("row_keep", [P, S], F32, YO + 24576)
        row_all = place("row_all", [P, S], F32, X + 3072)
        rot_c = place("rot_c", [P, 10, 32], F32, SCR)
        rot_s = place("rot_s", [P, 10, 32], F32, SCR + 1280)
        roped = place("roped", [P, 6, 2, 32], F32, SCR + 2560)
        q_t = place("q_t", [P, 2, P], F32, SCR + 4096)
        k_t = place("k_t", [P, S], F32, SCR + 5120)
        v_tok = place("v_tok", [P, NB, HD], F32, SCR + 9216)
        prob = place("prob", [P, 4, 2 * P], F32, SCR + 11264)
        prob_t = place("prob_t", [P, 2, 4 * P], F32, SCR + 15360)
        silu_az = place("silu_az", [P, 2, S], F32, SCR + 19456)
        y_hi = place("y_hi", [P, KT, S], F32R, SCR)
        sig_a = place("sig_a", [P, 2, HALF], F32, X)
        mix_a = place("mix_a", [P, 2, S], F32, X + 4096)
        mq_t = place("mq_t", [P, 2, S], F32, SCR)
        mk_t = place("mk_t", [P, 2, S], F32, SCR + 8192)
        gate_m = place("gate_m", [P, 2, S], F32, SCR + 16384)
        xpad = place("xpad", [P, CW - 1 + S], F32, SCR + 24576)
        conv = place("conv", [P, S], F32, SCR + 28704)
        num = place("num", [P, NB, MV], F32, SCR + 24576)
        dec = place("dec", [P, S + NB], F32, X + 64)
        state = place("state", [P, 2, MV], F32, X + 4224)
        v_aug = place("v_aug", [P, 2, MV], F32, X + 6304)
        k_w = place("k_w", [P, 2, MD], F32, X + 8384)
        s_dec = place("s_dec", [P, 2, P], F32, X + 10432)
        inter = place("inter", [P, MV], F32, X + 11456)
        sig_o = place("sig_o", [P, HALF], F32, X + 12512)
        sig_m = place("sig_m", [P, KT, S], F32, SCR)
        w_gate = place("w_gate", [P, 2, D], F32, X)
        gate_acc = place("gate_acc", [P, D], F32, X + 8192)
        y2_hi = place("y2_hi", [P, KT, S], F32R, HT)
        mix_in = place("mix_in", [P, 2, S], F32, X)
        merged = place("merged", [P, HALF], F32, X + 12288)
        g_hi = place("g_hi", [P, KT, S], F32R, SCR)
        g_lo = place("g_lo", [P, KT, S], F32R, HT + K32)
        w2_hi = place("w2_hi", [P, 4, KT, P], F32R, HT)
        w2_lo = place("w2_lo", [P, 4, KT, P], F32R, HT + 4 * 4096)
        res = place("res", [P, NB, D], F32, YO)
        fin_w = place("fin_w", [P, D], F32, X)
        gate_b = place("gate_b", [P, D], F32, X + 4096)
        gated = place("gated", [P, HALF], F32, X + 8192)

        pp = ctx.enter_context(nc.psum_tensor("pp", [P, 8, HALF], F32))

        def bank(b):
            return pp[:, b, :]

        vec_loaded, small_loaded, gate_row_loaded, dec_loaded = (
            sem("vec_loaded"), sem("small_loaded"), sem("gate_row_loaded"), sem("dec_loaded"))
        x_loaded = [sem(f"x_loaded{n}") for n in range(4)]
        mod_loaded = [sem(f"mod_loaded{n}") for n in range(KT)]
        slot_loaded = [sem(f"slot_loaded{s}") for s in range(5)]
        w_gate_loaded = [sem(f"w_gate_loaded{n}") for n in range(2)]
        mix_loaded = [sem(f"mix_loaded{n}") for n in range(2)]
        res_loaded = [sem(f"res_loaded{n}") for n in range(NB)]
        fin_loaded = sem("fin_loaded")
        row_stored, out_stored = sem("row_stored"), sem("out_stored")
        mix_stored = [counter(f"mix_stored{n}", 16) for n in range(2)]
        slot_hi = [counter(f"slot_hi{s}") for s in range(5)]
        slot_split = [counter(f"slot_split{s}") for s in range(5)]
        slot_free = [counter(f"slot_free{s}") for s in range(5)]
        bank_full = [counter(f"bank_full{b}") for b in range(2)]
        bank_free = [counter(f"bank_free{b}") for b in range(2)]
        consts_zeroed, consts_ready, gate_slot_zeroed = sem("consts_zeroed"), sem("consts_ready"), sem("gate_slot_zeroed")
        pos_converted, vecs_turned, pos_turned, vecs_ready = sem("pos_converted"), sem("vecs_turned"), sem("pos_turned"), sem("vecs_ready")
        angle_step, sin_ready, half_sin, rope_ready = sem("angle_step"), sem("sin_ready"), sem("half_sin"), sem("rope_ready")
        x_squared, x_rstd_step, x_normed = sem("x_squared"), sem("x_rstd_step"), sem("x_normed")
        x_turned, x_evac_act, x_evac_dve = sem("x_turned"), sem("x_evac_act"), sem("x_evac_dve")
        silu_c_ready, mod_summed, mod_cols, mod_step = sem("silu_c_ready"), sem("mod_summed"), sem("mod_cols"), sem("mod_step")
        h_modulated, h_hi_ready, h_lo_ready = sem("h_modulated"), sem("h_hi_ready"), sem("h_lo_ready")
        row_step, row_act, rows_turned, cols_step = sem("row_step"), sem("row_act"), sem("rows_turned"), sem("cols_step")
        head_sinks = counter("head_sinks")
        rope_product, rope_done, v_copied = counter("rope_product"), counter("rope_done"), counter("v_copied")
        qk_turned, qk_copied = counter("qk_turned"), counter("qk_copied")
        scores_full, max_done, neg_m_done, exp_done = (
            counter("scores_full"), counter("max_done"), counter("neg_m_done"), counter("exp_done"))
        den_step, probs_ready, probs_turned = counter("den_step"), counter("probs_ready"), counter("probs_turned")
        prob_t_old, prob_t_new = counter("prob_t_old"), counter("prob_t_new")
        att_full, att_copied, att_gated = counter("att_full"), counter("att_copied"), counter("att_gated")
        y_hi_ready, y_lo_ready, mix_ready = sem("y_hi_ready"), sem("y_lo_ready"), counter("mix_ready")
        head_set, mask_added, dec_ready = counter("head_set"), counter("mask_added"), counter("dec_ready")
        conv_step, conv_silu = counter("conv_step"), counter("conv_silu")
        k_turned, k_weighted, v_ready = counter("k_turned"), counter("k_weighted"), counter("v_ready")
        s_full, s_decayed = counter("s_full"), counter("s_decayed")
        inter_full, inter_ready, intra_full, num_ready = (
            counter("inter_full"), counter("inter_ready"), counter("intra_full"), counter("num_ready"))
        h_den_done, h_rec_done, h_squared = counter("h_den_done"), counter("h_rec_done"), counter("h_squared")
        kv_full, state_ready = counter("kv_full"), counter("state_ready")
        h_norm_step, h_rms_done, h_normed, h_turned = (
            counter("h_norm_step"), counter("h_rms_done"), counter("h_normed"), counter("h_turned"))
        gate_m_done, ym_ready = counter("gate_m_done"), counter("ym_ready")
        gate_sum = counter("gate_sum")
        y2_hi_ready, y2_lo_ready = sem("y2_hi_ready"), sem("y2_lo_ready")
        merge_product, merged_ready, g_hi_ready, g_lo_ready = (
            counter("merge_product"), counter("merged_ready"), counter("g_hi_ready"), counter("g_lo_ready"))
        gate_bias_added, gate_spread, gate_ready = sem("gate_bias_added"), sem("gate_spread"), sem("gate_ready")
        w2_hi_ready, w2_ready = sem("w2_hi_ready"), sem("w2_ready")
        gated_done, res_added, res_squared, o_step, o_rms_done, out_ready = (
            sem("gated_done"), sem("res_added"), sem("res_squared"), sem("o_step"), sem("o_rms_done"), sem("out_ready"))

        def unit(phase, per, i, e):
            return e % 2, before(BANK_USES, phase) + per * i + e // 2

        def use(phase, s, n):
            return before(SLOT_USES, phase, s) + n

        w_in_v = w_in.rearrange("(k p) c -> p k c", p=P)
        w_att_v = w_att.rearrange("(k p) c -> p k c", p=P)
        w_m_v = w_m.rearrange("(k p) c -> p k c", p=P)
        w_out_v = w_out.rearrange("(k p) c -> p k c", p=P)
        w_ada_v = w_ada.rearrange("(k p) c -> p k c", p=P)
        x_v = x.rearrange("(n p) d -> p n d", p=P)
        out_v = out.rearrange("(n p) d -> p n d", p=P)
        merged_v = merged_dram.rearrange("(k p) t -> p k t", p=P)

        block = ctx.enter_context(nc.Block())

        @block.sync
        def _(sp):
            for rows, v, n in ((V_C, c, 8), (V_NW, norm_w, 8), (V_SH, b_ada[0:D], 8), (V_SC, b_ada[D:2 * D], 8),
                               (V_CQ, conv_q, 32), (V_CK, conv_k, 32), (V_MN, m_norm_w, 8)):
                sp.dma_start(vec_rows[rows:rows + n, :], v.rearrange("(r p) -> r p", p=P)).then_inc(vec_loaded, 16)
            sp.dma_start(pos_i[:, :], positions.rearrange("(n p) -> n p", p=P)).then_inc(small_loaded, 16)
            sp.dma_start(freq[:, :], inv_freq[None, :].broadcast_to([P, HD // 2])).then_inc(small_loaded, 16)
            sp.dma_start(sink[:, :], att_sinks[None, :].broadcast_to([P, 16])).then_inc(small_loaded, 16)
            for q in range(2):
                sp.dma_start(bias_if[32 * q:32 * q + 4, :], b_if[4 * q:4 * q + 4, None]).then_inc(small_loaded, 16)
            for n in range(4):
                sp.dma_start(x_in[:, 2 * n:2 * n + 2, :], x_v[:, 2 * n:2 * n + 2, :]).then_inc(x_loaded[n], 16)
            for k in range(KT):
                sp.dma_start(w_mod[:, k, :], w_ada_v[:, k, 0:2 * D]).then_inc(mod_loaded[k], 16)

            sp.wait_ge(gate_slot_zeroed, 1)
            sp.dma_start(raw[:, 0, :, 0:4], w_in_v[:, :, MI:MI + 4]).then_inc(slot_loaded[0], 16)
            sp.dma_start(raw[:, 0, :, 32:36], w_in_v[:, :, MF:MF + 4]).then_inc(slot_loaded[0], 16)

            def load(src, s, uses):
                after(sp, slot_split[s], uses)
                sp.dma_start(raw[:, s, :, :], src).then_inc(slot_loaded[s], 16)

            with sp.Fori(0, KVH, 1) as i:
                for s in range(2):
                    src = w_in_v[:, :, bass.ds(sp.snap(AQ + s * P + i * 256), P)]
                    load(src, s, use("A", s, 0) + i)
                src_k = w_in_v[:, :, bass.ds(sp.snap(AK + i * HD), HD)]
                src_v = w_in_v[:, :, bass.ds(sp.snap(AV + i * HD), HD)]
                after(sp, slot_split[2], use("A", 2, 0) + i)
                sp.dma_start(raw[:, 2, :, 0:HD], src_k).then_inc(slot_loaded[2], 16)
                sp.dma_start(raw[:, 2, :, HD:P], src_v).then_inc(slot_loaded[2], 16)
                for s in range(3, 5):
                    src = w_in_v[:, :, bass.ds(sp.snap(AZ + (s - 3) * P + i * 256), P)]
                    load(src, s, use("A", s, 0) + i)

            with sp.Fori(0, 4, 1) as i:
                for k in range(2):
                    src = w_in_v[:, :, bass.ds(sp.snap(GA + k * P + i * 256), P)]
                    src_w = w_att_v[:, :, bass.ds(sp.snap(k * P + i * 256), P)]
                    after(sp, slot_split[2 * k + 1], use("B", 2 * k + 1, 0) + i)
                    sp.dma_start(raw[:, 2 * k, :, :], src).then_inc(slot_loaded[2 * k], 16)
                    sp.dma_start(raw[:, 2 * k + 1, :, :], src_w).then_inc(slot_loaded[2 * k + 1], 16)
                for k in range(2):
                    dst = merged_v[:, bass.ds(sp.snap(2 * i + k), 1), :]
                    after(sp, mix_ready, 4 * i + 2 * k + 2)
                    sp.dma_start(dst, mix_a[:, k:k + 1, :]).then_inc(mix_stored[k], 16)

            with sp.Fori(0, MH, 1) as i:
                for n, (col, s, k) in enumerate(C_LOADS):
                    src = w_in_v[:, :, bass.ds(sp.snap(col + i * MD), P)]
                    load(src, s, use("C", s, k) + 2 * i)
                    if n == C_MASK_AFTER - 1:
                        src = row_pack[bass.ds(sp.snap(i), 1), :].broadcast_to([P, S + NB])
                        after(sp, state_ready, 14 * i)
                        for b in range(2):
                            sp.wait_ge(mix_stored[b], 16 * 5)
                        sp.dma_start(dec[:, :], src).then_inc(dec_loaded, 16)

            with sp.Fori(0, 2, 1) as i:
                for s in range(4):
                    src = w_in_v[:, :, bass.ds(sp.snap(GM + s * P + i * 512), P)]
                    load(src, s, use("D1", s, 0) + i)

            with sp.Fori(0, 2, 1) as i:
                for s in range(4):
                    src = w_m_v[:, :, bass.ds(sp.snap(s * P + i * 512), P)]
                    load(src, s, use("D2", s, 0) + i)
                    src = merged_v[:, bass.ds(sp.snap(4 * i + s), 1), :]
                    sp.wait_ge(gate_bias_added, 1)
                    after(sp, merged_ready, 8 * i + 2 * s - 2 if s >= 1 else 8 * i)
                    sp.dma_start(mix_in[:, s % 2:s % 2 + 1, :], src).then_inc(mix_loaded[s % 2], 16)

            for s in range(4):
                load(w_out_v[:, :, s * P:(s + 1) * P], s, use("E", s, 0))
            after(sp, merged_ready, 16)
            sp.dma_start(fin_w[:, :], final_norm_w[None, :].broadcast_to([P, D])).then_inc(fin_loaded, 16)
            for b in range(2):
                after(sp, bank_full[b], before(BANK_USES, "E"))
            for n in range(NB):
                sp.dma_start(res[:, n, :], x_v[:, n, :]).then_inc(res_loaded[n], 16)
            for s in range(4):
                load(w_out_v[:, :, HALF + s * P:HALF + (s + 1) * P], s, use("E2", s, 0))
            for n in range(NB):
                sp.wait_ge(out_ready, n + 1)
                sp.dma_start(out_v[:, n, :], res[:, n, :]).then_inc(out_stored, 16)
            sp.wait_ge(out_stored, 16 * NB)

        @block.gpsimd
        def _(pool):
            for s, start in counters:
                pool.nop().then_inc(s, start)
            pool.memset(ones[:, :], 1.0).then_inc(consts_zeroed, 1)
            pool.memset(ident[:, :], 0.0).then_inc(consts_zeroed, 1)
            pool.memset(ident_bf[:, :], 0.0).then_inc(consts_zeroed, 1)
            pool.memset(causal[:, :], 0.0).then_inc(consts_zeroed, 1)
            pool.memset(band[:, :], 0.0).then_inc(consts_zeroed, 1)
            pool.memset(neg_half[:, :], -0.5).then_inc(consts_zeroed, 1)
            pool.memset(raw[:, 0, :, :], 0.0).then_inc(gate_slot_zeroed, 1)
            pool.wait_ge(consts_zeroed, 6)
            for m in (ident, ident_bf):
                pool.affine_select(out=m[:, :], in_=m[:, :], compare_op=ALU.not_equal, fill=1.0, base=0,
                                   pattern=[[-1, P]], channel_multiplier=1).then_inc(consts_ready, 1)
            pool.affine_select(out=causal[:, :], in_=causal[:, :], compare_op=ALU.is_ge, fill=NEG, base=0,
                               pattern=[[1, P]], channel_multiplier=-1).then_inc(consts_ready, 1)
            pool.affine_select(out=band[:, :], in_=band[:, :], compare_op=ALU.is_ge, fill=NEG, base=P,
                               pattern=[[-1, 2 * P]], channel_multiplier=1).then_inc(consts_ready, 1)
            pool.wait_ge(consts_ready, 4)
            pool.affine_select(out=band[:, :], in_=band[:, :], compare_op=ALU.is_ge, fill=NEG, base=-1,
                               pattern=[[1, 2 * P]], channel_multiplier=-1).then_inc(consts_ready, 1)
            pool.wait_ge(consts_ready, 5)
            pool.affine_select(out=band0[:, :], in_=band[:, :], compare_op=ALU.is_ge, fill=NEG, base=-P,
                               pattern=[[1, 2 * P]], channel_multiplier=0).then_inc(consts_ready, 1)

            pool.wait_ge(x_squared, NB)
            pool.tensor_scalar(x_ssq[:, :], x_ssq[:, :], 1.0 / D, EPS, ALU.mult, ALU.add).then_inc(x_rstd_step, 1)
            pool.wait_ge(x_rstd_step, 1)
            pool.tensor_tensor(x_rstd[:, :], x_ssq[:, :], neg_half[:, :], ALU.pow).then_inc(x_rstd_step, 1)

            one = ones[:, 0:1, None].broadcast_to([P, KT, P])

            def split(s, uses, loads, hi=None, lo=None):
                if hi is None:
                    after(pool, slot_free[s], uses)
                hi = w_hi[:, s, :, :] if hi is None else hi
                lo = w_lo[:, s, :, :] if lo is None else lo
                pool.wait_ge(slot_loaded[s], 16 * loads)
                pool.tensor_tensor(hi, raw[:, s, :, :], one, ALU.mult).then_inc(slot_hi[s], 1)
                after(pool, slot_hi[s], uses + 1)
                pool.tensor_tensor(lo, raw[:, s, :, :], hi.bitcast(F32), ALU.subtract).then_inc(slot_split[s], 1)

            def loads(phase, s, n):
                return before(SLOT_DMAS, phase, s) + n

            split(0, use("G", 0, 0), loads("G", 0, 2))
            with pool.Fori(0, KVH, 1) as i:
                for s in range(5):
                    per = 2 if s == 2 else 1
                    split(s, use("A", s, 0) + i, loads("A", s, per) + per * i)
            with pool.Fori(0, 4, 1) as i:
                for s in range(4):
                    split(s, use("B", s, 0) + i, loads("B", s, 1) + i)
            with pool.Fori(0, MH, 1) as i:
                for n, (_, s, k) in enumerate(C_LOADS):
                    split(s, use("C", s, k) + 2 * i, loads("C", s, k + 1) + 2 * i)
                    if n == C_MASK_AFTER - 1:
                        pool.wait_ge(dec_loaded, 16 * (i + 1))
                        d = dec[:, 0:S].rearrange("p (n t) -> p n t", n=NB)
                        pool.tensor_tensor(d, d, causal[:, None, :].broadcast_to([P, NB, P]), ALU.add).then_inc(mask_added, 1)
            for phase in ("D1", "D2"):
                with pool.Fori(0, 2, 1) as i:
                    for s in range(4):
                        split(s, use(phase, s, 0) + i, loads(phase, s, 1) + i)
            for s in range(4):
                split(s, use("E", s, 0), loads("E", s, 1))
            for b in range(2):
                after(pool, bank_full[b], before(BANK_USES, "E"))
            for s in range(4):
                split(s, use("E2", s, 0), loads("E2", s, 1), hi=w2_hi[:, s, :, :], lo=w2_lo[:, s, :, :])

        @block.tensor
        def _(pe):
            def passes(o, lhs, rhs, k, first, last):
                (lh, ll), (rh, rl) = lhs, rhs
                pe.matmul(o, lh, rh, start=first, stop=False)
                pe.matmul(o, lh, rl, start=False, stop=False)
                return pe.matmul(o, ll, rh, start=False, stop=last)

            def feature_unit(phase, per, i, e, s, half, src_hi, src_lo, ready=None):
                b, n = unit(phase, per, i, e)
                after(pe, bank_free[b], n)
                t = slice(half * HALF, (half + 1) * HALF)
                for k in range(KT):
                    if ready is not None:
                        pe.wait_ge(ready, k + 1)
                    ins = passes(bank(b), (w_hi[:, s, k, :], w_lo[:, s, k, :]),
                                 (src_hi[:, k, t], src_lo[:, k, t]), k, k == 0, k == KT - 1)
                ins.then_inc(bank_full[b], 1)

            def token_unit(phase, per, i, e, blk, wh, wl, n_slots):
                b, n = unit(phase, per, i, e)
                after(pe, bank_free[b], n)
                t = slice(blk * P, (blk + 1) * P)
                o = bank(b)[:, 0:n_slots * P].rearrange("p (s c) -> p s c", s=n_slots)
                for k in range(KT):
                    ins = passes(o, (h_hi[:, k, t], h_lo[:, k, t]), (wh[:, :, k, :], wl[:, :, k, :]), k, k == 0, k == KT - 1)
                ins.then_inc(bank_full[b], 1)

            def release(s, phase, per, i, e):
                b, n = unit(phase, per, i, e)
                after(pe, bank_free[b], n)
                pe.matmul(bank(b)[:, 0:2], ident_bf[:, :], ident_bf[:, 0:2], start=True, stop=True).then_inc(slot_free[s], 1)

            pe.wait_ge(consts_ready, 2)
            pe.wait_ge(vec_loaded, 16 * 7)
            pe.transpose(bank(2)[:, 0:V_N], vec_rows[:, :], ident[0:V_N, 0:V_N]).then_inc(vecs_turned, 1)
            pe.wait_ge(pos_converted, 1)
            pe.transpose(bank(3)[:, 0:NB], pos_f[:, :], ident[0:NB, 0:NB]).then_inc(pos_turned, 1)
            for q in range(16):
                half, k = q // 8, q % 8
                b = 4 + q % 4
                if k == 0:
                    pe.wait_ge(x_normed, 4 * half + 4)
                if q >= 4:
                    pe.wait_ge(x_evac_act if q % 2 == 0 else x_evac_dve, (q - 4) // 2 + 1)
                for n in range(4):
                    ins = pe.transpose(bank(b)[:, n * P:(n + 1) * P], x_in[:, 4 * half + n, k * P:(k + 1) * P], ident[:, :])
                ins.then_inc(x_turned, 1)
            pe.wait_ge(mod_summed, KT)
            for f in range(16):
                ins = pe.matmul(bank(3)[:, 16 + f:17 + f], mod_acc[:, f * P:(f + 1) * P], ones[:, 0:1], start=True, stop=True)
            ins.then_inc(mod_cols, 1)

            after(pe, slot_split[0], use("G", 0, 1))
            for half in range(2):
                feature_unit("G", 1, 0, half, 0, half, h_hi, h_lo, ready=h_lo_ready)
            release(0, "G", 1, 0, 2)

            pe.wait_ge(consts_ready, 6)

            def turn_qk(i, m):
                pe_o = bank(2)
                after(pe, rope_done, 2 * (NB * i + m + 1))
                after(pe, qk_copied, 2 * (NB * i + m))
                for pair in range(2):
                    pe.transpose(pe_o[:, pair * P:(pair + 1) * P], roped[:, 2 * pair:2 * pair + 2, :, :], ident[:, :])
                pe.transpose(pe_o[:, 2 * P:3 * P], roped[:, 4:6, :, :], ident[:, :]).then_inc(qk_turned, 1)

            def scores(i, m):
                after(pe, qk_copied, 2 * (NB * i + m + 1))
                after(pe, exp_done, 5 * (NB * i + m))
                mask = (band if m else band0)[:, None, :].broadcast_to([P, 2, 2 * P])
                for odd in range(2):
                    pe.matmul(bank(3 + odd).rearrange("p (a k) -> p a k", a=2), ident_bf[:, :], mask, start=True, stop=True)
                    part = slice(odd * HD, (odd + 1) * HD)
                    for pair in range(2):
                        k0 = P if m == 0 else 0
                        keys = slice(max(m - 1, 0) * P, (m + 1) * P)
                        ins = pe.matmul(bank(3 + odd)[:, pair * 2 * P + k0:(pair + 1) * 2 * P], q_t[part, pair, :],
                                        k_t[part, keys], start=False, stop=True, skip_group_check=True)
                ins.then_inc(scores_full, 1)

            def turn_probs(i, m):
                after(pe, probs_ready, 4 * (NB * i + m + 1))
                if m >= 2:
                    after(pe, prob_t_old, 7 * i + m - 1)
                elif m == 0:
                    after(pe, prob_t_old, 7 * i)
                after(pe, prob_t_new, NB * i + m)
                for old in range(1 if m == 0 else 0, 2):
                    for g in range(4):
                        ins = pe.transpose(bank(5 + old)[:, g * P:(g + 1) * P], prob[:, g, old * P:(old + 1) * P], ident[:, :])
                ins.then_inc(probs_turned, 1)

            def weigh_v(i, m):
                if m:
                    after(pe, prob_t_old, 7 * i + m)
                after(pe, prob_t_new, NB * i + m + 1)
                after(pe, v_copied, NB * i + m + 1)
                after(pe, att_copied, NB * i + m)
                for odd in range(2):
                    for old in range(1 if m == 0 else 0, 2):
                        ins = pe.matmul(pp[odd * HD:(odd + 1) * HD, 7, 0:2 * P], v_tok[:, m - 1 + old, :],
                                        prob_t[:, old, odd * 2 * P:(odd + 1) * 2 * P],
                                        start=(old == (1 if m == 0 else 0)), stop=(old == 1), skip_group_check=True)
                ins.then_inc(att_full, 1)

            with pe.Fori(0, KVH, 1) as i:
                for u in range(12):
                    if u < NB:
                        if u == 0:
                            for s in range(3):
                                after(pe, slot_split[s], use("A", s, 1) + i)
                        token_unit("A", 6, i, u, u, w_hi[:, 0:3], w_lo[:, 0:3], 3)
                        if u == NB - 1:
                            for s in range(3):
                                release(s, "A", 6, i, u + 1)
                    else:
                        s = 3 + (u - NB) // 2
                        if u % 2 == 0:
                            after(pe, slot_split[s], use("A", s, 1) + i)
                        feature_unit("A", 6, i, u, s, u % 2, h_hi, h_lo)
                        if u % 2:
                            release(s, "A", 6, i, u + 1)
                    if 1 <= u <= NB:
                        turn_qk(i, u - 1)
                    if 3 <= u <= NB + 2:
                        turn_probs(i, u - 3)
                    if 2 <= u <= NB + 1:
                        scores(i, u - 2)
                    if 4 <= u:
                        weigh_v(i, u - 4)

            pe.wait_ge(row_act, 5)
            after(pe, qk_copied, 2 * NB * KVH)
            after(pe, exp_done, 5 * NB * KVH)
            for n in range(NB):
                ins = pe.transpose(bank(2 + n // 4)[:, (n % 4) * P:(n % 4 + 1) * P], row_all[:, n * P:(n + 1) * P], ident[:, :])
            ins.then_inc(rows_turned, 1)

            with pe.Fori(0, 4, 1) as i:
                for k in range(2):
                    after(pe, slot_split[2 * k], use("B", 2 * k, 1) + i)
                    for half in range(2):
                        feature_unit("B", 4, i, 4 * k + half, 2 * k, half, h_hi, h_lo)
                    release(2 * k, "B", 4, i, 4 * k + 2)
                    after(pe, slot_split[2 * k + 1], use("B", 2 * k + 1, 1) + i)
                    for half in range(2):
                        feature_unit("B", 4, i, 4 * k + 2 + half, 2 * k + 1, half, y_hi, y_lo, ready=y_lo_ready)
                    release(2 * k + 1, "B", 4, i, 4 * k + 4)

            def turn_k(i, n):
                if n == 0:
                    after(pe, conv_silu, 4 * (i + 1))
                    after(pe, ym_ready, 4 * i)
                    pe.wait_ge(cols_step, 3)
                else:
                    after(pe, k_weighted, NB * i + n)
                for f in range(2):
                    ins = pe.transpose(bank(2)[:, f * P:(f + 1) * P], mk_t[:, f, n * P:(n + 1) * P], ident[:, :])
                ins.then_inc(k_turned, 1)

            def key_query(i, n):
                after(pe, s_decayed, NB * i + n)
                for f in range(2):
                    t = slice(n * P, (n + 1) * P)
                    ins = pe.matmul(bank(3)[:, 0:P], mk_t[:, f, t], mq_t[:, f, t], start=(f == 0), stop=(f == 1))
                ins.then_inc(s_full, 1)

            def chunk(i, n):
                if n:
                    after(pe, state_ready, 14 * i + 2 * n)
                    after(pe, inter_ready, 7 * i + n - 1 if n > 1 else 7 * i)
                    for f in range(2):
                        ins = pe.matmul(bank(4)[:, 0:MV], mq_t[:, f, n * P:(n + 1) * P], state[:, f, :], start=(f == 0), stop=(f == 1))
                    ins.then_inc(inter_full, 1)
                after(pe, s_decayed, NB * i + n + 1)
                after(pe, v_ready, NB * i + n + 1)
                after(pe, num_ready, NB * i + n)
                pe.matmul(bank(5)[:, 0:MV], s_dec[:, n % 2, :], v_aug[:, n % 2, :], start=True, stop=True).then_inc(intra_full, 1)
                if n < NB - 1:
                    after(pe, k_weighted, NB * i + n + 1)
                    after(pe, state_ready, 14 * i + 2 * n)
                    for f in range(2):
                        ins = pe.matmul(bank(6 + f)[:, 0:MV], k_w[:, n % 2, f * P:(f + 1) * P], v_aug[:, n % 2, :], start=True, stop=True)
                    ins.then_inc(kv_full, 1)

            c_slot = {"mq0": (0, 0), "mq1": (1, 0), "mk0": (2, 0), "mk1": (3, 0), "mz0": (4, 0), "mz1": (2, 1),
                      "mo0": (3, 1), "mo1": (4, 1)}
            with pe.Fori(0, MH, 1) as i:
                for e, (kind, n) in enumerate(C_UNITS):
                    if kind == "mv":
                        if n == 0:
                            for s in range(2):
                                after(pe, slot_split[s], use("C", s, 2) + 2 * i)
                        token_unit("C", 12, i, e, n, w_hi[:, 0:2], w_lo[:, 0:2], 2)
                        if n == NB - 1:
                            release(0, "C", 12, i, e + 1)
                            release(1, "C", 12, i, e + 1)
                        turn_k(i, n)
                        key_query(i, n)
                    else:
                        s, k = c_slot[f"{kind}{n // 2}"]
                        if n % 2 == 0:
                            after(pe, slot_split[s], use("C", s, k + 1) + 2 * i)
                        feature_unit("C", 12, i, e, s, n % 2, h_hi, h_lo)
                        if n % 2:
                            release(s, "C", 12, i, e + 1)
                    if kind == "mv" and n >= 1:
                        chunk(i, n - 1)
                    if (kind, n) == ("mo", 0):
                        chunk(i, NB - 1)
                    if (kind, n) == ("mo", 2):
                        after(pe, k_weighted, NB * (i + 1))
                        for q in range(4):
                            f, half = q // 2, q % 2
                            after(pe, h_normed, NB * i + 4 * half + 4)
                            for m in range(4):
                                ins = pe.transpose(bank(2 + q)[:, m * P:(m + 1) * P], num[:, 4 * half + m, f * P:(f + 1) * P], ident[:, :])
                            ins.then_inc(h_turned, 1)

            for phase, hi, lo, ready in (("D1", h_hi, h_lo, None), ("D2", y2_hi, y_lo, y2_lo_ready)):
                with pe.Fori(0, 2, 1) as i:
                    for s in range(4):
                        after(pe, slot_split[s], use(phase, s, 1) + i)
                        for half in range(2):
                            feature_unit(phase, 4, i, 2 * s + half, s, half, hi, lo, ready=ready)
                        release(s, phase, 4, i, 2 * s + 2)

            pe.wait_ge(gate_bias_added, 1)
            for half in range(2):
                ins = pe.matmul(bank(6 + half), ones[:, :], gate_acc[:, half * HALF:(half + 1) * HALF], start=True, stop=True)
            ins.then_inc(gate_spread, 1)
            after(pe, g_lo_ready, 16)
            for half in range(2):
                for s in range(4):
                    if half == 0:
                        after(pe, slot_split[s], use("E", s, 1))
                    else:
                        after(pe, slot_split[s], use("E2", s, 1))
                wh, wl = (w_hi[:, 0:4], w_lo[:, 0:4]) if half == 0 else (w2_hi[:, :], w2_lo[:, :])
                for n in range(NB):
                    b, uses = unit("E", 8, 0, half * NB + n)
                    after(pe, bank_free[b], uses)
                    o = bank(b).rearrange("p (s c) -> p s c", s=4)
                    t = slice(n * P, (n + 1) * P)
                    for k in range(KT):
                        ins = passes(o, (g_hi[:, k, t], g_lo[:, k, t]), (wh[:, :, k, :], wl[:, :, k, :]), k, k == 0, k == KT - 1)
                    ins.then_inc(bank_full[b], 1)

        @block.scalar
        def _(act):
            def full(phase, per, i, e):
                b, n = unit(phase, per, i, e)
                after(act, bank_full[b], n + 1)
                return b

            act.wait_ge(vecs_ready, 1)
            act.activation(silu_c[:, :], vecs[:, V_C:V_C + KT], ACT.Silu).then_inc(silu_c_ready, 1)
            junk = pp[:, 0:2, :].rearrange("p b c -> p (b c)")
            for n in range(NB):
                act.wait_ge(x_loaded[n // 2], 16)
                if n:
                    act.wait_ge(x_squared, n)
                act.activation(junk, x_in[:, n, :], ACT.Square, accum_out=x_ssq[:, n:n + 1]).then_inc(x_squared, 1)
            act.wait_ge(angle_step, 9)
            act.activation(sin[:, :, :], ang[:, :, :], ACT.Sin).then_inc(sin_ready, 1)
            act.activation(turns[:, :, :], ang[:, :, :], ACT.Sin, scale=0.5).then_inc(half_sin, 1)
            for q in range(0, 16, 2):
                half, k = q // 8, q % 8
                act.wait_ge(x_turned, q + 1)
                act.activation(xnt[:, k, half * HALF:(half + 1) * HALF], bank(4 + q % 4), ACT.Copy).then_inc(x_evac_act, 1)
            for k in range(KT):
                act.wait_ge(h_modulated, k + 1)
                act.activation(h_hi[:, k, :], xnt[:, k, :], ACT.Copy).then_inc(h_hi_ready, 1)

            act.wait_ge(row_step, 5)
            act.activation(row_e[32:36, :], row_e[32:36, :], ACT.Exp).then_inc(row_act, 1)
            act.wait_ge(row_act, 1)
            act.activation(row_e[32:36, :], row_e[32:36, :], ACT.Ln, bias=1.0).then_inc(row_act, 1)
            act.wait_ge(row_step, 11)
            act.activation(row_all[96:100, :], row_m[0:4, :], ACT.Exp, scale=-1.0).then_inc(row_act, 1)
            act.wait_ge(row_step, 15)
            act.activation(row_all[64:68, :], row_all[64:68, :], ACT.Exp).then_inc(row_act, 1)
            act.activation(row_all[32:36, :], row_all[32:36, :], ACT.Exp).then_inc(row_act, 1)
            act.wait_ge(row_act, 5)
            act.dma_start(row_pack[:, 0:S], row_c[0:4, :]).then_inc(row_stored, 16)
            act.dma_start(row_pack[:, S:S + NB], row_all[32:36, P - 1:S:P],
                          allow_slow_non_contiguous=True).then_inc(row_stored, 16)

            def copy_qk(i, m):
                after(act, qk_turned, NB * i + m + 1)
                after(act, scores_full, NB * i + m)
                act.activation(q_t[:, :, :], bank(2)[:, 0:2 * P].rearrange("p (a t) -> p a t", a=2), ACT.Copy).then_inc(qk_copied, 1)
                act.activation(k_t[:, m * P:(m + 1) * P], bank(2)[:, 2 * P:3 * P], ACT.Copy).then_inc(qk_copied, 1)

            def exponentials(i, m):
                after(act, neg_m_done, 2 * (NB * i + m + 1))
                after(act, probs_turned, NB * i + m)
                for g in range(4):
                    s = bank(3 + g // 2)[:, (g % 2) * 2 * P:(g % 2 + 1) * 2 * P]
                    act.activation(prob[:, g, :], s, ACT.Exp, bias=neg_m[:, g:g + 1], scale=ATT_SCALE,
                                   accum_out=p_sum[:, g:g + 1]).then_inc(exp_done, 1)
                act.activation(sink_e[:, :], sink_d[:, :], ACT.Exp).then_inc(exp_done, 1)

            def copy_old_probs(i, m):
                after(act, probs_turned, NB * i + m + 1)
                after(act, att_full, NB * i + m)
                act.activation(prob_t[:, 0, :], bank(5), ACT.Copy).then_inc(prob_t_old, 1)

            with act.Fori(0, KVH, 1) as i:
                for u in range(13):
                    if 2 <= u <= NB + 1:
                        copy_qk(i, u - 2)
                    if 5 <= u <= NB + 3:
                        copy_old_probs(i, u - 4)
                    if 3 <= u <= NB + 2:
                        exponentials(i, u - 3)
                    if u >= 9:
                        e = u - 1
                        b = full("A", 6, i, e)
                        after(act, att_gated, i)
                        half = e % 2
                        act.activation(silu_az[:, (e - NB) // 2, half * HALF:(half + 1) * HALF], bank(b), ACT.Silu).then_inc(bank_free[b], 1)

            after(act, att_gated, KVH)
            for k in range(KT):
                act.activation(y_hi[:, k, :], y[:, k, :], ACT.Copy).then_inc(y_hi_ready, 1)
            with act.Fori(0, 4, 1) as i:
                for k in range(2):
                    for half in range(2):
                        b = full("B", 4, i, 4 * k + half)
                        after(act, mix_ready, 4 * i + 2 * k)
                        act.activation(sig_a[:, half, :], bank(b), ACT.Sigmoid).then_inc(bank_free[b], 1)

            with act.Fori(0, MH, 1) as i:
                after(act, head_set, i + 1)
                for e, (kind, n) in enumerate(C_UNITS):
                    b = full("C", 12, i, e)
                    cols_half = slice((n % 2) * HALF, (n % 2 + 1) * HALF)
                    if kind in ("mq", "mk"):
                        f = n // 2 + (2 if kind == "mk" else 0)
                        if n % 2 == 0:
                            after(act, conv_step, 4 * (4 * i + f))
                            after(act, h_turned, 4 * i)
                        act.activation(xpad[:, CW - 1 + (n % 2) * HALF:CW - 1 + (n % 2 + 1) * HALF], bank(b), ACT.Copy).then_inc(bank_free[b], 1)
                        if n % 2:
                            after(act, conv_step, 4 * (4 * i + f + 1))
                            dst = (mk_t if kind == "mk" else mq_t)[:, n // 2, :]
                            act.activation(dst, conv[:, :], ACT.Silu).then_inc(conv_silu, 1)
                        if (kind, n) == ("mk", 3):
                            after(act, mask_added, i + 1)
                            for m in range(NB):
                                act.activation(dec[:, m * P:(m + 1) * P], dec[:, m * P:(m + 1) * P], ACT.Exp,
                                               bias=h_cols[:, m, 0:1]).then_inc(dec_ready, 1)
                    if kind == "mv":
                        if n >= 2:
                            after(act, intra_full, NB * i + n - 1)
                            after(act, kv_full, 7 * i + n - 1)
                        act.activation(v_aug[:, n % 2, 0:MD], bank(b)[:, 0:MD], ACT.Copy).then_inc(v_ready, 1)
                        after(act, v_ready, NB * i + n + 1)
                        after(act, k_turned, NB * i + n + 1)
                        act.activation(k_w[:, n % 2, :], bank(2)[:, 0:MD], ACT.Copy, scale=h_cols[:, n, 2:3]).then_inc(k_weighted, 1)
                        act.nop().then_inc(bank_free[b], 1)
                    if kind == "mz":
                        after(act, ym_ready, 4 * i)
                        act.activation(gate_m[:, n // 2, cols_half], bank(b), ACT.Silu).then_inc(bank_free[b], 1)
                    if kind == "mo":
                        after(act, gate_m_done, 4 * i + n)
                        act.activation(sig_o[:, :], bank(b), ACT.Sigmoid).then_inc(bank_free[b], 1)
                    m = n - 1 if kind == "mv" else NB - 1
                    if (kind == "mv" and n >= 1) or (kind, n) == ("mo", 0):
                        if m:
                            after(act, inter_full, 7 * i + m)
                            after(act, h_squared, NB * i + m)
                            after(act, num_ready, NB * i + m)
                            act.activation(inter[:, :], bank(4)[:, 0:MV], ACT.Copy, scale=h_cols[:, m, 1:2]).then_inc(inter_ready, 1)
                        after(act, h_rec_done, NB * i + m + 1)
                        act.activation(inter[:, 0:MD], num[:, m, 0:MD], ACT.Square, scale=h_rec[:, m:m + 1],
                                       accum_out=h_ssq[:, m:m + 1]).then_inc(h_squared, 1)
                    if (kind, n) == ("mo", 0):
                        after(act, h_norm_step, 3 * i + 1)
                        act.activation(h_rms[:, :], h_ms[:, :], ACT.Sqrt).then_inc(h_rms_done, 1)

            after(act, ym_ready, 4 * MH)
            with act.Fori(0, 2, 1) as i:
                for s in range(4):
                    src = w_ada_v[:, bass.ds(4 * i + s, 1), 2 * D:3 * D]
                    after(act, gate_sum, 4 * i + s - 1 if s >= 1 else 4 * i)
                    act.dma_start(w_gate[:, s % 2:s % 2 + 1, :], src).then_inc(w_gate_loaded[s % 2], 16)
                    for half in range(2):
                        b = full("D1", 4, i, 2 * s + half)
                        dst = sig_m[:, bass.ds(4 * i + s, 1), half * HALF:(half + 1) * HALF]
                        act.activation(dst, bank(b)[:, None, :], ACT.Sigmoid).then_inc(bank_free[b], 1)
            after(act, gate_sum, KT)
            act.dma_start(w_gate[0:1, 0, :], b_ada[None, 2 * D:3 * D]).then_inc(gate_row_loaded, 16)
            for b in range(2):
                after(act, bank_full[b], before(BANK_USES, "D2"))
            for k in range(KT):
                act.activation(y2_hi[:, k, :], y[:, k, :], ACT.Copy).then_inc(y2_hi_ready, 1)
            with act.Fori(0, 2, 1) as i:
                for s in range(4):
                    for half in range(2):
                        n = 8 * i + 2 * s + half
                        after(act, merged_ready, n + 1)
                        dst = g_hi[:, bass.ds(4 * i + s, 1), half * HALF:(half + 1) * HALF]
                        act.activation(dst, merged[:, None, :], ACT.Copy).then_inc(g_hi_ready, 1)

            for half in range(2):
                for n in range(NB):
                    e = half * NB + n
                    act.wait_ge(res_added, e + 1)
                    if e:
                        act.wait_ge(res_squared, e)
                    act.activation(bank(2), res[:, n, half * HALF:(half + 1) * HALF], ACT.Square,
                                   accum_out=o_ssq[:, n, half:half + 1]).then_inc(res_squared, 1)
                    if half:
                        act.wait_ge(o_step, 3 * n + 2)
                        act.activation(o_rms[:, n:n + 1], o_ms[:, n:n + 1], ACT.Sqrt).then_inc(o_rms_done, 1)

        @block.vector
        def _(dve):
            def full(phase, per, i, e):
                b, n = unit(phase, per, i, e)
                after(dve, bank_full[b], n + 1)
                return b

            dve.wait_ge(small_loaded, 16 * 5)
            dve.tensor_copy(pos_f[:, :], pos_i[:, :]).then_inc(pos_converted, 1)
            dve.tensor_scalar(neg_sink[:, :], sink[:, :], -1.0, None, ALU.mult).then_inc(angle_step, 1)
            dve.wait_ge(vecs_turned, 1)
            dve.tensor_copy(vecs[:, :], bank(2)[:, 0:V_N]).then_inc(vecs_ready, 1)
            dve.wait_ge(pos_turned, 1)
            dve.tensor_copy(pos_col[:, :], bank(3)[:, 0:NB]).then_inc(angle_step, 1)
            dve.wait_ge(angle_step, 2)
            shape = [P, NB, HD // 2]
            dve.tensor_tensor(ang[:, :, :], pos_col[:, :, None].broadcast_to(shape), freq[:, None, :].broadcast_to(shape),
                              ALU.mult).then_inc(angle_step, 1)
            dve.wait_ge(angle_step, 3)
            dve.tensor_scalar(turns[:, :, :], ang[:, :, :], 1.0 / TWO_PI, None, ALU.mult).then_inc(angle_step, 1)
            dve.wait_ge(angle_step, 4)
            dve.tensor_copy(turns_i[:, :, :], turns[:, :, :]).then_inc(rope_ready, 1)
            dve.wait_ge(rope_ready, 1)
            dve.tensor_copy(turns[:, :, :], turns_i[:, :, :]).then_inc(rope_ready, 1)
            dve.wait_ge(rope_ready, 2)
            for n, part in enumerate((PI_A, PI_B, PI_C1, PI_C2)):
                dve.wait_ge(angle_step, 4 + n)
                dve.scalar_tensor_tensor(out=ang[:, :, :], in0=turns[:, :, :], scalar=-part, in1=ang[:, :, :],
                                         op0=ALU.mult, op1=ALU.add).then_inc(angle_step, 1)
            dve.wait_ge(angle_step, 8)
            dve.tensor_scalar(ang[:, :, :], ang[:, :, :], PI_TOP, -PI_TOP, ALU.min, ALU.max).then_inc(angle_step, 1)
            dve.wait_ge(half_sin, 1)
            dve.tensor_tensor(turns[:, :, :], turns[:, :, :], turns[:, :, :], ALU.mult).then_inc(rope_ready, 1)
            dve.wait_ge(rope_ready, 3)
            dve.tensor_scalar(cos[:, :, :], turns[:, :, :], -2.0, 1.0, ALU.mult, ALU.add).then_inc(rope_ready, 1)
            dve.wait_ge(x_rstd_step, 2)
            for n in range(NB):
                dve.tensor_scalar(x_in[:, n, :], x_in[:, n, :], x_rstd[:, n:n + 1], None, ALU.mult).then_inc(x_normed, 1)
            for q in range(1, 16, 2):
                half, k = q // 8, q % 8
                dve.wait_ge(x_turned, q + 1)
                dve.tensor_copy(xnt[:, k, half * HALF:(half + 1) * HALF], bank(4 + q % 4)).then_inc(x_evac_dve, 1)
            dve.wait_ge(silu_c_ready, 1)
            for k in range(KT):
                dve.wait_ge(mod_loaded[k], 16)
                if k == 0:
                    dve.tensor_scalar(mod_acc[:, :], w_mod[:, 0, :], silu_c[:, 0:1], None, ALU.mult).then_inc(mod_summed, 1)
                else:
                    dve.wait_ge(mod_summed, k)
                    dve.scalar_tensor_tensor(out=mod_acc[:, :], in0=w_mod[:, k, :], scalar=silu_c[:, k:k + 1], in1=mod_acc[:, :],
                                             op0=ALU.mult, op1=ALU.add).then_inc(mod_summed, 1)
            dve.wait_ge(mod_cols, 1)
            dve.tensor_tensor(shift[:, :], bank(3)[:, 16:24], vecs[:, V_SH:V_SH + KT], ALU.add).then_inc(mod_step, 1)
            dve.tensor_tensor(scale_t[:, :], bank(3)[:, 24:32], vecs[:, V_SC:V_SC + KT], ALU.add).then_inc(mod_step, 1)
            dve.wait_ge(mod_step, 2)
            dve.scalar_tensor_tensor(out=scale1[:, :], in0=scale_t[:, :], scalar=1.0, in1=vecs[:, V_NW:V_NW + KT],
                                     op0=ALU.add, op1=ALU.mult).then_inc(mod_step, 1)
            dve.wait_ge(mod_step, 3)
            dve.wait_ge(x_evac_act, 8)
            dve.wait_ge(x_evac_dve, 8)
            for k in range(KT + 1):
                if k < KT:
                    dve.tensor_scalar(xnt[:, k, :], xnt[:, k, :], scale1[:, k:k + 1], shift[:, k:k + 1], ALU.mult, ALU.add).then_inc(h_modulated, 1)
                if k:
                    dve.wait_ge(h_hi_ready, k)
                    dve.tensor_tensor(h_lo[:, k - 1, :], xnt[:, k - 1, :], h_hi[:, k - 1, :].bitcast(F32), ALU.subtract).then_inc(h_lo_ready, 1)

            dve.memset(row_all[:, :], 0.0).then_inc(row_step, 1)
            for half in range(2):
                b = full("G", 1, 0, half)
                t = slice(half * HALF, (half + 1) * HALF)
                dve.tensor_scalar(row_if[0:4, t], bank(b)[0:4, :], bias_if[0:4, :], None, ALU.add).then_inc(row_step, 1)
                dve.tensor_scalar(row_if[32:36, t], bank(b)[32:36, :], bias_if[32:36, :], None, ALU.add).then_inc(bank_free[b], 1)
            for b in range(2):
                after(dve, bank_free[b], 1)
            dve.memset(row_keep[0:4, :], 1.0).then_inc(row_step, 1)
            dve.scalar_tensor_tensor(out=row_e[32:36, :], in0=row_if[32:36, :], scalar=-1.0, in1=row_if[32:36, :],
                                     op0=ALU.mult, op1=ALU.min).then_inc(row_step, 1)
            dve.wait_ge(row_step, 5)
            dve.memset(row_keep[0:4, 0:S:P], 0.0).then_inc(row_step, 1)
            dve.memset(m_prev[:, :], 0.0).then_inc(row_step, 1)
            dve.wait_ge(row_act, 2)
            dve.scalar_tensor_tensor(out=row_logf[0:4, :], in0=row_if[32:36, :], scalar=0.0, in1=row_e[32:36, :],
                                     op0=ALU.min, op1=ALU.subtract).then_inc(row_step, 1)
            dve.wait_ge(row_step, 8)
            dve.tensor_tensor_scan(out=row_b[0:4, :], data0=row_keep[0:4, :], data1=row_logf[0:4, :], initial=0.0,
                                   op0=ALU.mult, op1=ALU.add).then_inc(row_step, 1)
            dve.wait_ge(row_step, 9)
            dve.tensor_tensor(row_all[0:4, :], row_if[0:4, :], row_b[0:4, :], ALU.subtract).then_inc(row_step, 1)
            dve.tensor_tensor_scan(out=row_m[0:4, :], data0=row_logf[0:4, :], data1=row_if[0:4, :], initial=0.0,
                                   op0=ALU.add, op1=ALU.max).then_inc(row_step, 1)
            dve.wait_ge(row_step, 11)
            dve.tensor_tensor(row_c[0:4, :], row_b[0:4, :], row_m[0:4, :], ALU.subtract).then_inc(row_step, 1)
            dve.tensor_copy(m_prev[:, 1:NB], row_m[0:4, P - 1:S - P:P]).then_inc(row_step, 1)
            dve.wait_ge(row_step, 13)
            c3 = row_c[0:4, :].rearrange("h (n t) -> h n t", n=NB)
            a3 = row_all[0:4, :].rearrange("h (n t) -> h n t", n=NB)
            dve.tensor_tensor(row_all[32:36, :].rearrange("h (n t) -> h n t", n=NB), c3,
                              m_prev[:, :, None].broadcast_to([4, NB, P]), ALU.add).then_inc(row_step, 1)
            dve.tensor_tensor(row_all[64:68, :].rearrange("h (n t) -> h n t", n=NB), a3,
                              c3[:, :, P - 1:P].broadcast_to([4, NB, P]), ALU.add).then_inc(row_step, 1)

            def softmax_max(i, m):
                after(dve, scores_full, NB * i + m + 1)
                after(dve, neg_m_done, 2 * (NB * i + m))
                dve.tensor_reduce(s_max[:, :], pp[:, 3:5, :].rearrange("p b (a k) -> p (b a) k", a=2), AX.X, ALU.max).then_inc(max_done, 1)
                after(dve, max_done, NB * i + m + 1)
                after(dve, exp_done, 5 * (NB * i + m))
                dve.scalar_tensor_tensor(out=neg_m[:, :], in0=s_max[:, :], scalar=-ATT_SCALE,
                                         in1=h_neg_sink[:, :, :].rearrange("p b a -> p (b a)"),
                                         op0=ALU.mult, op1=ALU.min).then_inc(neg_m_done, 1)
                after(dve, neg_m_done, 2 * (NB * i + m) + 1)
                dve.tensor_tensor(sink_d[:, :], neg_m[:, :], h_neg_sink[:, :, :].rearrange("p b a -> p (b a)"),
                                  ALU.subtract).then_inc(neg_m_done, 1)

            def rope(i, m):
                b = full("A", 6, i, m)
                qk = bank(b)[:, 0:5 * HD].rearrange("p (h d) -> p h d", d=32)
                tab = [P, 10, 32]
                after(dve, att_full, NB * i)
                dve.tensor_copy(v_tok[:, m, :], bank(b)[:, 5 * HD:6 * HD]).then_inc(v_copied, 1)
                dve.tensor_tensor(rot_c[:, :, :], qk, cos[:, m:m + 1, :].broadcast_to(tab), ALU.mult).then_inc(rope_product, 1)
                dve.tensor_tensor(rot_s[:, :, :], qk, sin[:, m:m + 1, :].broadcast_to(tab), ALU.mult).then_inc(rope_product, 1)
                after(dve, rope_product, 2 * (NB * i + m + 1))
                after(dve, qk_turned, NB * i + m)
                pc = rot_c[:, :, :].rearrange("p (h a) d -> p h a d", a=2)
                ps = rot_s[:, :, :].rearrange("p (h a) d -> p h a d", a=2)
                dve.tensor_tensor(roped[:, 0:5, 0, :], pc[:, :, 0, :], ps[:, :, 1, :], ALU.subtract).then_inc(bank_free[b], 1)
                dve.tensor_tensor(roped[:, 0:5, 1, :], pc[:, :, 1, :], ps[:, :, 0, :], ALU.add).then_inc(rope_done, 1)
                after(dve, rope_done, 2 * (NB * i + m) + 1)
                after(dve, bank_free[b], unit("A", 6, i, m)[1] + 1)
                dve.tensor_copy(roped[:, 5, :, :], roped[:, 4, :, :]).then_inc(rope_done, 1)

            def normalise(i, m):
                after(dve, exp_done, 5 * (NB * i + m + 1))
                dve.tensor_tensor(p_den[:, :], p_sum[:, :], sink_e[:, :], ALU.add).then_inc(den_step, 1)
                after(dve, den_step, 2 * (NB * i + m) + 1)
                dve.reciprocal(p_rec[:, :], p_den[:, :]).then_inc(den_step, 1)
                after(dve, den_step, 2 * (NB * i + m) + 2)
                for g in range(4):
                    dve.tensor_scalar(prob[:, g, :], prob[:, g, :], p_rec[:, g:g + 1], None, ALU.mult).then_inc(probs_ready, 1)

            def copy_new_probs(i, m):
                after(dve, probs_turned, NB * i + m + 1)
                after(dve, att_full, NB * i + m)
                dve.tensor_copy(prob_t[:, 1, :], bank(6)).then_inc(prob_t_new, 1)

            def copy_att(i, m):
                after(dve, att_full, NB * i + m + 1)
                dst = y[:, bass.ds(2 * i, 2), m * P:(m + 1) * P]
                dve.tensor_scalar(dst, bank(7)[:, 0:2 * P].rearrange("p (a t) -> p a t", a=2), 1.0, None, ALU.mult).then_inc(att_copied, 1)

            dve.wait_ge(row_stored, 32)
            with dve.Fori(0, KVH, 1) as i:
                src = neg_sink[:, bass.ds(4 * i, 4)].rearrange("p (a b) -> p b a", b=2)
                dve.tensor_scalar(h_neg_sink[:, :, :], src, 1.0, None, ALU.mult).then_inc(head_sinks, 1)
                after(dve, head_sinks, i + 1)
                for u in range(13):
                    if 3 <= u <= NB + 2:
                        softmax_max(i, u - 3)
                    if 1 <= u <= NB:
                        rope(i, u - 1)
                    if 4 <= u <= NB + 3:
                        copy_new_probs(i, u - 4)
                    if 5 <= u:
                        copy_att(i, u - 5)
                    if 3 <= u <= NB + 2:
                        normalise(i, u - 3)
                for e in (10, 11):
                    b, n = unit("A", 6, i, e)
                    after(dve, bank_free[b], n + 1)
                after(dve, att_copied, NB * (i + 1))
                dst = y[:, bass.ds(2 * i, 2), :]
                dve.tensor_tensor(dst, dst, silu_az[:, :, :], ALU.mult).then_inc(att_gated, 1)

            after(dve, att_gated, KVH)
            for k in range(KT):
                dve.wait_ge(y_hi_ready, k + 1)
                dve.tensor_tensor(y_lo[:, k, :], y[:, k, :], y_hi[:, k, :].bitcast(F32), ALU.subtract).then_inc(y_lo_ready, 1)
            dve.wait_ge(rows_turned, 1)
            for n in range(2):
                src = bank(2 + n).rearrange("p (n q h) -> p n q h", n=4, q=4)[:, :, :, 0:4].rearrange("p n q h -> p q h n")
                for q in range(4):
                    ins = dve.tensor_copy(cols[:, :, 4 * n:4 * n + 4, q], src[:, q, :, :])
                ins.then_inc(cols_step, 1)
            dve.wait_ge(cols_step, 2)
            dve.tensor_scalar(cols[:, :, :, 2], cols[:, :, :, 2], K_SCALE, None, ALU.mult).then_inc(cols_step, 1)
            with dve.Fori(0, 4, 1) as i:
                for k in range(2):
                    for half in range(2):
                        b0, n0 = unit("B", 4, i, 4 * k + half)
                        after(dve, bank_free[b0], n0 + 1)
                        if half == 0:
                            dve.wait_ge(mix_stored[k], 16 * (i + 1))
                        b = full("B", 4, i, 4 * k + 2 + half)
                        after(dve, mix_ready, 4 * i + 2 * k + half)
                        dve.tensor_tensor(mix_a[:, k, half * HALF:(half + 1) * HALF], sig_a[:, half, :], bank(b),
                                          ALU.mult).then_inc(mix_ready, 1)
                        after(dve, mix_ready, 4 * i + 2 * k + half + 1)
                        dve.nop().then_inc(bank_free[b], 1)

            for b in range(2):
                dve.wait_ge(mix_stored[b], 16 * 5)
            dve.wait_ge(cols_step, 3)
            dve.memset(v_aug[:, :, MD:MV], 1.0).then_inc(cols_step, 1)

            def decay_scores(i, n):
                after(dve, s_full, NB * i + n + 1)
                after(dve, dec_ready, NB * i + n + 1)
                if n >= 2:
                    after(dve, intra_full, NB * i + n - 1)
                dve.scalar_tensor_tensor(out=s_dec[:, n % 2, :], in0=bank(3)[:, 0:P], scalar=K_SCALE,
                                         in1=dec[:, n * P:(n + 1) * P], op0=ALU.mult, op1=ALU.mult).then_inc(s_decayed, 1)

            def numerator(i, n):
                after(dve, intra_full, NB * i + n + 1)
                if n == 0:
                    dve.tensor_copy(num[:, 0, :], bank(5)[:, 0:MV]).then_inc(num_ready, 1)
                else:
                    after(dve, inter_ready, 7 * i + n)
                    dve.tensor_tensor(num[:, n, :], inter[:, :], bank(5)[:, 0:MV], ALU.add).then_inc(num_ready, 1)
                if n < NB - 1:
                    after(dve, kv_full, 7 * i + n + 1)
                    for f in range(2):
                        if n == 0:
                            dve.tensor_copy(state[:, f, :], bank(6 + f)[:, 0:MV]).then_inc(state_ready, 1)
                        else:
                            after(dve, state_ready, 14 * i + 2 * n + f)
                            dve.scalar_tensor_tensor(out=state[:, f, :], in0=state[:, f, :], scalar=dec[:, S + n:S + n + 1],
                                                     in1=bank(6 + f)[:, 0:MV], op0=ALU.mult, op1=ALU.add).then_inc(state_ready, 1)
                after(dve, num_ready, NB * i + n + 1)
                dve.tensor_tensor(h_den[:, n:n + 1], num[:, n, MD:MV], h_cols[:, n, 3:4], ALU.max).then_inc(h_den_done, 1)
                after(dve, h_den_done, 2 * (NB * i + n) + 1)
                dve.scalar_tensor_tensor(out=h_den[:, n:n + 1], in0=num[:, n, MD:MV], scalar=-1.0, in1=h_den[:, n:n + 1],
                                         op0=ALU.mult, op1=ALU.max).then_inc(h_den_done, 1)
                after(dve, h_den_done, 2 * (NB * i + n + 1))
                dve.reciprocal(h_rec[:, n:n + 1], h_den[:, n:n + 1]).then_inc(h_rec_done, 1)

            with dve.Fori(0, MH, 1) as i:
                after(dve, dec_ready, NB * i)
                after(dve, h_squared, NB * i)
                after(dve, k_weighted, NB * i)
                after(dve, h_turned, 4 * i)
                dve.tensor_scalar(h_cols[:, :, :], cols[:, bass.ds(i, 1), :, :].rearrange("p h n q -> p (h n) q"), 1.0, None, ALU.mult)
                for taps, row in ((taps_q, V_CQ), (taps_k, V_CK)):
                    for j in range(CW):
                        dve.tensor_scalar(taps[:, j, :], vecs[:, bass.ds(row + KT * j + 2 * i, 2)], 1.0, None, ALU.mult)
                dve.tensor_scalar(m_norm[:, :], vecs[:, bass.ds(V_MN + 2 * i, 2)], 1.0, None, ALU.mult)
                dve.memset(xpad[:, 0:CW - 1], 0.0).then_inc(head_set, 1)
                after(dve, head_set, i + 1)
                for e, (kind, n) in enumerate(C_UNITS):
                    b, uses = unit("C", 12, i, e)
                    if kind in ("mq", "mk") and n % 2:
                        f = n // 2 + (2 if kind == "mk" else 0)
                        taps = taps_k if kind == "mk" else taps_q
                        after(dve, bank_free[0], unit("C", 12, i, e - 1)[1] + 1 if b == 1 else uses + 1)
                        after(dve, bank_free[1], uses + 1 if b == 1 else unit("C", 12, i, e - 1)[1] + 1)
                        after(dve, conv_silu, 4 * i + f)
                        for j in range(CW):
                            if j == 0:
                                dve.tensor_scalar(conv[:, :], xpad[:, 0:S], taps[:, 0, n // 2:n // 2 + 1], None, ALU.mult).then_inc(conv_step, 1)
                            else:
                                after(dve, conv_step, 4 * (4 * i + f) + j)
                                dve.scalar_tensor_tensor(out=conv[:, :], in0=xpad[:, j:j + S], scalar=taps[:, j, n // 2:n // 2 + 1],
                                                         in1=conv[:, :], op0=ALU.mult, op1=ALU.add).then_inc(conv_step, 1)
                    if kind == "mv":
                        decay_scores(i, n)
                        if n >= 1:
                            numerator(i, n - 1)
                    if (kind, n) == ("mo", 0):
                        numerator(i, NB - 1)
                        after(dve, h_squared, NB * (i + 1))
                        dve.tensor_scalar(h_ms[:, :], h_ssq[:, :], 1.0 / MD, EPS, ALU.mult, ALU.add).then_inc(h_norm_step, 1)
                        after(dve, h_rms_done, i + 1)
                        dve.reciprocal(h_inv[:, :], h_rms[:, :]).then_inc(h_norm_step, 1)
                        after(dve, h_norm_step, 3 * i + 2)
                        dve.tensor_tensor(h_scale[:, :], h_inv[:, :], h_rec[:, :], ALU.mult).then_inc(h_norm_step, 1)
                        after(dve, h_norm_step, 3 * i + 3)
                        for m in range(NB):
                            dve.tensor_scalar(num[:, m, 0:MD], num[:, m, 0:MD], h_scale[:, m:m + 1], None, ALU.mult).then_inc(h_normed, 1)
                    if kind == "mo":
                        after(dve, bank_free[b], uses + 1)
                        g = gate_m[:, n // 2, (n % 2) * HALF:(n % 2 + 1) * HALF]
                        dve.scalar_tensor_tensor(out=g, in0=g, scalar=m_norm[:, n // 2:n // 2 + 1], in1=sig_o[:, :],
                                                 op0=ALU.mult, op1=ALU.mult).then_inc(gate_m_done, 1)
                for q in range(4):
                    f, half = q // 2, q % 2
                    after(dve, h_turned, 4 * i + q + 1)
                    after(dve, gate_m_done, 4 * (i + 1))
                    dst = y[:, bass.ds(2 * i + f, 1), half * HALF:(half + 1) * HALF]
                    dve.tensor_tensor(dst, bank(2 + q)[:, None, :], gate_m[:, f:f + 1, half * HALF:(half + 1) * HALF], ALU.mult).then_inc(ym_ready, 1)

            after(dve, ym_ready, 4 * MH)
            dve.memset(gate_acc[:, :], 0.0).then_inc(cols_step, 1)
            dve.wait_ge(cols_step, 5)
            with dve.Fori(0, 2, 1) as i:
                for s in range(4):
                    dve.wait_ge(w_gate_loaded[s % 2], 16 * (2 * i + s // 2 + 1))
                    after(dve, gate_sum, 4 * i + s)
                    dve.scalar_tensor_tensor(out=gate_acc[:, :], in0=w_gate[:, s % 2, :], scalar=silu_c[:, bass.ds(4 * i + s, 1)],
                                             in1=gate_acc[:, :], op0=ALU.mult, op1=ALU.add).then_inc(gate_sum, 1)
            dve.wait_ge(gate_row_loaded, 16)
            after(dve, gate_sum, KT)
            dve.tensor_tensor(gate_acc[0:1, :], gate_acc[0:1, :], w_gate[0:1, 0, :], ALU.add).then_inc(gate_bias_added, 1)
            for k in range(KT):
                dve.wait_ge(y2_hi_ready, k + 1)
                dve.tensor_tensor(y_lo[:, k, :], y[:, k, :], y2_hi[:, k, :].bitcast(F32), ALU.subtract).then_inc(y2_lo_ready, 1)
            with dve.Fori(0, 2, 1) as i:
                for s in range(4):
                    for half in range(2):
                        n = 8 * i + 2 * s + half
                        t = slice(half * HALF, (half + 1) * HALF)
                        b = full("D2", 4, i, 2 * s + half)
                        after(dve, g_lo_ready, n)
                        dve.tensor_tensor(merged[:, None, :], sig_m[:, bass.ds(4 * i + s, 1), t], bank(b)[:, None, :], ALU.mult).then_inc(bank_free[b], 1)
                        dve.wait_ge(mix_loaded[s % 2], 16 * (2 * i + s // 2 + 1))
                        after(dve, bank_free[b], unit("D2", 4, i, 2 * s + half)[1] + 1)
                        dve.tensor_tensor(merged[:, :], merged[:, :], mix_in[:, s % 2, t], ALU.add).then_inc(merged_ready, 1)
                        after(dve, g_hi_ready, n + 1)
                        dve.tensor_tensor(g_lo[:, bass.ds(4 * i + s, 1), t], merged[:, None, :],
                                          g_hi[:, bass.ds(4 * i + s, 1), t].bitcast(F32), ALU.subtract).then_inc(g_lo_ready, 1)

            dve.wait_ge(gate_spread, 1)
            after(dve, merged_ready, 16)
            dve.tensor_copy(gate_b[:, :], pp[:, 6:8, :].rearrange("p b c -> p (b c)")).then_inc(gate_ready, 1)
            dve.wait_ge(gate_ready, 1)
            dve.wait_ge(fin_loaded, 16)
            for half in range(2):
                for n in range(NB):
                    e = half * NB + n
                    t = slice(half * HALF, (half + 1) * HALF)
                    b = full("E", 8, 0, e)
                    if e:
                        dve.wait_ge(res_added, e)
                    dve.tensor_tensor(gated[:, :], bank(b), gate_b[:, t], ALU.mult).then_inc(bank_free[b], 1)
                    dve.wait_ge(res_loaded[n], 16)
                    after(dve, bank_free[b], unit("E", 8, 0, e)[1] + 1)
                    dve.tensor_tensor(res[:, n, t], res[:, n, t], gated[:, :], ALU.add).then_inc(res_added, 1)
                    if half:
                        dve.wait_ge(res_squared, e + 1)
                        dve.tensor_tensor(o_sum[:, n:n + 1], o_ssq[:, n, 0:1], o_ssq[:, n, 1:2], ALU.add).then_inc(o_step, 1)
                        dve.wait_ge(o_step, 3 * n + 1)
                        dve.tensor_scalar(o_ms[:, n:n + 1], o_sum[:, n:n + 1], 1.0 / D, EPS, ALU.mult, ALU.add).then_inc(o_step, 1)
                        dve.wait_ge(o_rms_done, n + 1)
                        dve.reciprocal(o_rstd[:, n:n + 1], o_rms[:, n:n + 1]).then_inc(o_step, 1)
                        dve.wait_ge(o_step, 3 * n + 3)
                        dve.scalar_tensor_tensor(out=res[:, n, :], in0=res[:, n, :], scalar=o_rstd[:, n:n + 1], in1=fin_w[:, :],
                                                 op0=ALU.mult, op1=ALU.mult).then_inc(out_ready, 1)


def kernel(x, c, positions, w_ada, b_ada, norm_w, w_in, b_if, att_sinks, conv_q, conv_k,
           m_norm_w, w_att_branch, w_m_branch, w_out, final_norm_w):
    import numpy as _np
    import concourse.bacc as _bacc
    from concourse import mybir as _mybir
    from concourse.bass_utils import run_bass_kernel_spmd as _run

    nc = _bacc.Bacc("TRN2", target_bir_lowering=False, num_devices=1)
    freqs = (_np.float32(10000.0) ** (-_np.arange(0, HD, 2, dtype=_np.float32) / _np.float32(HD))).astype(_np.float32)
    arrays = {
        "x": _np.ascontiguousarray(x).reshape(S, D),
        "c": _np.ascontiguousarray(c).reshape(D),
        "positions": _np.ascontiguousarray(positions).reshape(S),
        "w_ada": _np.ascontiguousarray(w_ada).reshape(D, 3 * D),
        "b_ada": _np.ascontiguousarray(b_ada).reshape(3 * D),
        "norm_w": _np.ascontiguousarray(norm_w).reshape(D),
        "w_in": _np.ascontiguousarray(w_in).reshape(D, GM + D),
        "b_if": _np.ascontiguousarray(b_if).reshape(2 * MH),
        "att_sinks": _np.ascontiguousarray(att_sinks).reshape(16),
        "conv_q": _np.ascontiguousarray(conv_q).reshape(CW * D),
        "conv_k": _np.ascontiguousarray(conv_k).reshape(CW * D),
        "m_norm_w": _np.ascontiguousarray(m_norm_w).reshape(D),
        "w_att": _np.ascontiguousarray(w_att_branch).reshape(D, D),
        "w_m": _np.ascontiguousarray(w_m_branch).reshape(D, D),
        "w_out": _np.ascontiguousarray(w_out).reshape(D, D),
        "final_norm_w": _np.ascontiguousarray(final_norm_w).reshape(D),
        "inv_freq": freqs,
    }
    aps = {n: nc.dram_tensor(n, a.shape, _mybir.dt.from_np(a.dtype), kind="ExternalInput").ap() for n, a in arrays.items()}
    f32 = _mybir.dt.float32
    out = nc.dram_tensor("out", (S, D), f32, kind="ExternalOutput").ap()
    row_pack = nc.dram_tensor("row_pack", (MH, S + NB), f32, kind="Internal").ap()
    merged_dram = nc.dram_tensor("merged_dram", (D, S), f32, kind="Internal").ap()
    build(nc, out=out, row_pack=row_pack, merged_dram=merged_dram, **aps)
    r = _run(nc, [arrays], core_ids=[0])
    return r.results[0]["out"].reshape(1, S, D)
```

```python
from contextlib import ExitStack

import numpy as np

import concourse.bass as bass
from concourse import mybir

F32 = mybir.dt.float32
F32R = mybir.dt.float32r
BF16 = mybir.dt.bfloat16
I32 = mybir.dt.int32
ALU = mybir.AluOpType
ACT = mybir.ActivationFunctionType
AX = mybir.AxisListType

P = 128
D = 1024
S = 1024
KT = D // P
NB = S // P
HALF = 512
HD = 64
KVH = 4
MH = 4
MD = 256
MV = MD + 1
CW = 4
EPS = 1e-6
NEG = -1e30
ATT_SCALE = HD ** -0.5
K_SCALE = MD ** -0.5
(AQ, AK, AV, AZ, MQ, MK, MVC, MO, MZ, MI, MF, GA, GM) = np.cumsum(
    [0, 1024, 256, 256, 1024, 1024, 1024, 1024, 1024, 1024, 4, 4, 1024]).tolist()
V_C, V_NW, V_SH, V_SC, V_CQ, V_CK, V_MN, V_N = 0, 8, 16, 24, 32, 64, 96, 104
TWO_PI = 6.283185307179586
PI_A = 6.25
PI_B = 0.033203125
PI_C = TWO_PI - PI_A - PI_B
PI_C1 = float(np.float32(round(PI_C * 2 ** 24) / 2 ** 24))
PI_C2 = PI_C - PI_C1
PI_TOP = 3.1415925

SLOT_USES = {"G": (0, 0, 0, 0, 1), "A": (4,) * 5, "B": (4, 4, 4, 4, 0), "C": (8,) * 5,
             "D1": (2, 2, 2, 0, 2), "D2": (2, 2, 2, 0, 2), "E": (1, 1, 1, 1, 0), "E2": (1, 1, 1, 1, 0)}
SLOT_DMAS = {"G": (0, 0, 0, 0, 2), "A": (4, 4, 8, 4, 4), "B": (4, 4, 4, 4, 0), "C": (8,) * 5,
             "D1": (2, 2, 2, 0, 2), "D2": (2, 2, 2, 0, 2), "E": (1, 1, 1, 1, 0), "E2": (1, 1, 1, 1, 0)}
D_SLOTS = (0, 1, 2, 4)
BANK_USES = {"A": 24, "B": 16, "C": 48, "D1": 8, "D2": 8, "E": 8}


def before(table, phase, slot=None):
    total = 0
    for name, n in table.items():
        if name == phase:
            return total
        total += n if slot is None else n[slot]


C_UNITS = [("mq", 0), ("mq", 1), ("mq", 2), ("mq", 3), ("mk", 0), ("mk", 1), ("mk", 2), ("mk", 3)]
for _u in range(NB):
    if _u % 2 == 0:
        C_UNITS.append(("mz", _u // 2))
    C_UNITS.append(("mv", _u))
C_UNITS += [("mo", 0), ("mo", 1), ("mo", 2), ("mo", 3)]
C_LOADS = [(MQ, 0, 0), (MQ + P, 1, 0), (MK, 2, 0), (MK + P, 3, 0), (MZ, 4, 0),
           (MVC, 0, 1), (MVC + P, 1, 1), (MZ + P, 2, 1), (MO, 3, 1), (MO + P, 4, 1)]
MOD_BY_ACT = (1, 4, 7)
C_SLOT = {"mq0": (0, 0), "mq1": (1, 0), "mk0": (2, 0), "mk1": (3, 0), "mz0": (4, 0), "mz1": (2, 1),
          "mo0": (3, 1), "mo1": (4, 1)}
C_MASK_AFTER = 2


def build(nc, x, c, positions, w_ada, b_ada, norm_w, w_in, b_if, att_sinks, conv_q, conv_k,
          m_norm_w, w_att, w_m, w_out, final_norm_w, inv_freq, out, row_pack, merged_dram):
    with ExitStack() as ctx:
        counters = []

        def sb(name, shape, dt=F32):
            return ctx.enter_context(nc.sbuf_tensor(name, shape, dt))

        def sem(name):
            return ctx.enter_context(nc.semaphore(name))

        def counter(name, start=1):
            s = sem(name)
            counters.append((s, start))
            return s

        def after(eng, s, n):
            eng.wait_ge(s, n + 1)

        ident = sb("ident", [P, P])
        ones = sb("ones", [P, P])
        causal = sb("causal", [P, P])
        vec_rows = sb("vec_rows", [V_N, P])
        vecs = sb("vecs", [P, V_N])
        silu_c = sb("silu_c", [P, KT])
        pos_i = sb("pos_i", [NB, P], I32)
        pos_f = sb("pos_f", [NB, P])
        pos_col = sb("pos_col", [P, NB])
        freq = sb("freq", [P, HD // 2])
        sink = sb("sink", [P, 16])
        neg_sink = sb("neg_sink", [P, 16])
        bias_if = sb("bias_if", [36, 1])
        scale1 = sb("scale1", [P, KT])
        scale_t = sb("scale_t", [P, KT])
        shift = sb("shift", [P, KT])
        x_ssq = sb("x_ssq", [P, NB])
        x_rstd = sb("x_rstd", [P, NB])
        neg_half = sb("neg_half", [P, NB])
        m_prev = sb("m_prev", [4, NB])
        cols = sb("cols", [P, MH, NB, 4])
        h_cols = sb("h_cols", [P, NB, 4])
        taps_q = sb("taps_q", [P, CW, 2])
        taps_k = sb("taps_k", [P, CW, 2])
        m_norm = sb("m_norm", [P, 2])
        h_neg_sink = sb("h_neg_sink", [P, 2, 2])
        s_max = sb("s_max", [P, 4])
        neg_m = sb("neg_m", [P, 4])
        sink_d = sb("sink_d", [P, 4])
        p_sum = sb("p_sum", [P, 4])
        sink_e = sb("sink_e", [P, 4])
        p_den = sb("p_den", [P, 4])
        p_rec = sb("p_rec", [P, 4])
        h_den = sb("h_den", [P, NB])
        h_rec = sb("h_rec", [P, NB])
        h_ssq = sb("h_ssq", [P, NB])
        h_ms = sb("h_ms", [P, NB])
        h_rms = sb("h_rms", [P, NB])
        h_inv = sb("h_inv", [P, NB])
        h_scale = sb("h_scale", [P, NB])
        o_ssq = sb("o_ssq", [P, NB, 2])
        o_sum = sb("o_sum", [P, NB])
        o_ms = sb("o_ms", [P, NB])
        o_rms = sb("o_rms", [P, NB])
        o_rstd = sb("o_rstd", [P, NB])

        base = (nc.sbuf_base + 63) // 64 * 64
        at = {}

        def place(name, shape, dt, offset):
            at[name] = offset
            return nc.alloc_sbuf_tensor_at(name, shape, dt, offset=base + offset)

        K32 = KT * S * 4
        HT, RAW = 0, 2 * K32
        WHI, WLO = RAW + 5 * 4096, RAW + 10 * 4096
        YO = WLO + 5 * 4096
        SCR = YO + K32
        X = SCR + K32
        h_hi = place("h_hi", [P, KT, S], F32R, HT)
        h_lo = place("h_lo", [P, KT, S], F32R, HT + K32)
        raw = place("raw", [P, 5, KT, P], F32, RAW)
        w_hi = place("w_hi", [P, 5, KT, P], F32R, WHI)
        w_lo = place("w_lo", [P, 5, KT, P], F32R, WLO)
        y = place("y", [P, KT, S], F32, YO)
        y_lo = place("y_lo", [P, KT, S], F32R, YO)
        w_mod = place("w_mod", [P, KT, 2 * D], F32, HT)
        x_in = place("x_in", [P, NB, D], F32, YO)
        xnt = place("xnt", [P, KT, S], F32, SCR)
        x_mod = place("x_mod", [P, KT, S], F32, YO)
        cos = place("cos", [P, NB, HD // 2], F32, X)
        sin = place("sin", [P, NB, HD // 2], F32, X + 1024)
        later = place("later", [P, P], BF16, X + 2048)
        turned_old = place("turned_old", [P, P], BF16, X + 2304)
        turned_new = place("turned_new", [P, P], BF16, X + 2560)
        neg_col = place("neg_col", [P, 1], F32, X + 2816)
        mod_acc = place("mod_acc", [P, 2 * D], F32, X + 3072)
        ang = place("ang", [P, NB, HD // 2], F32, X + 11264)
        turns = place("turns", [P, NB, HD // 2], F32, X + 12288)
        turns_i = place("turns_i", [P, NB, HD // 2], I32, X + 13312)
        mod_col = place("mod_col", [P, 2 * KT], F32, X + 14336)
        row_if, row_e, row_logf, row_b, row_m, row_c = (
            place(name, [P, S], F32, YO + 8192 + 4096 * n)
            for n, name in enumerate(("row_if", "row_e", "row_logf", "row_b", "row_m", "row_c")))
        row_all = place("row_all", [P, S], F32, X + 3072)
        row_keep = row_e
        roped = place("roped", [P, 2, 6, 2, 32], F32, X + 7168)
        ident_r = place("ident_r", [P, P], F32R, X + 10240)
        rot_c = place("rot_c", [P, 10, 32], F32, X + 11264)
        rot_s = place("rot_s", [P, 10, 32], F32, X + 12544)
        q_parts = place("q_parts", [P, 2, 4, 2, HD], F32R, SCR)
        q_t = place("q_t", [P, 4, P], F32R, SCR + 4096)
        k_hi = place("k_hi", [P, S], F32R, SCR + 6144)
        k_lo = place("k_lo", [P, S], F32R, SCR + 10240)
        v_tok = place("v_tok", [P, NB, HD], F32, SCR + 14336)
        prob = place("prob", [P, 4, P], F32, SCR + 16384)
        prob_t = place("prob_t", [P, 2, 4 * P], F32, SCR + 20480)
        silu_az = place("silu_az", [P, 2, S], F32, SCR + 24576)
        y_hi = place("y_hi", [P, KT, S], F32R, SCR)
        sig_a = place("sig_a", [P, 2, HALF], F32, X)
        mix_a = place("mix_a", [P, 2, S], F32, X + 4096)
        mq_t = place("mq_t", [P, 2, S], F32, SCR)
        mk_t = place("mk_t", [P, 2, S], F32, SCR + 8192)
        gate_m = place("gate_m", [P, 2, S], F32, SCR + 16384)
        xpad = place("xpad", [P, CW - 1 + S], F32, SCR + 24576)
        conv = place("conv", [P, S], F32, SCR + 28704)
        num = place("num", [P, NB, MV], F32, SCR + 24576)
        dec = place("dec", [P, S + NB], F32, X + 64)
        state = place("state", [P, 2, MV], F32, X + 4224)
        v_aug = place("v_aug", [P, 2, MV], F32, X + 6304)
        k_w = place("k_w", [P, 2, MD], F32, X + 8384)
        s_dec = place("s_dec", [P, 2, P], F32, X + 10432)
        inter = place("inter", [P, MV], F32, X + 11456)
        sig_o = place("sig_o", [P, HALF], F32, X + 12512)
        sig_m = place("sig_m", [P, KT, S], F32, SCR)
        w_gate = place("w_gate", [P, 2, D], F32, X)
        gate_row = place("gate_row", [P, D], F32, RAW + 3 * 4096)
        gate_acc = place("gate_acc", [P, D], F32, X + 8192)
        y2_hi = place("y2_hi", [P, KT, S], F32R, HT)
        mix_in = place("mix_in", [P, 2, S], F32, X)
        merged = place("merged", [P, HALF], F32, X + 12288)
        g_hi = place("g_hi", [P, KT, S], F32R, SCR)
        g_lo = place("g_lo", [P, KT, S], F32R, HT + K32)
        w2_hi = place("w2_hi", [P, 4, KT, P], F32R, HT)
        w2_lo = place("w2_lo", [P, 4, KT, P], F32R, HT + 4 * 4096)
        res = place("res", [P, NB, D], F32, YO)
        fin_w = place("fin_w", [P, D], F32, X)
        gate_b = place("gate_b", [P, D], F32, X + 4096)
        gated = place("gated", [P, HALF], F32, X + 8192)

        pp = ctx.enter_context(nc.psum_tensor("pp", [P, 8, HALF], F32))

        def bank(b):
            return pp[:, b, :]

        vec_loaded, small_loaded, gate_row_loaded, dec_loaded = (
            sem("vec_loaded"), sem("small_loaded"), sem("gate_row_loaded"), sem("dec_loaded"))
        x_loaded = [sem(f"x_loaded{n}") for n in range(4)]
        mod_loaded = [sem(f"mod_loaded{n}") for n in range(KT + 1)]
        slot_loaded = [sem(f"slot_loaded{s}") for s in range(5)]
        w_gate_loaded = [sem(f"w_gate_loaded{n}") for n in range(2)]
        mix_loaded = [sem(f"mix_loaded{n}") for n in range(2)]
        res_loaded = [sem(f"res_loaded{n}") for n in range(NB)]
        fin_loaded = sem("fin_loaded")
        row_stored, out_stored = sem("row_stored"), sem("out_stored")
        mix_stored = [counter(f"mix_stored{n}", 16) for n in range(2)]
        slot_hi = [counter(f"slot_hi{s}") for s in range(5)]
        slot_split = [counter(f"slot_split{s}") for s in range(5)]
        slot_free = [counter(f"slot_free{s}") for s in range(5)]
        bank_full = [counter(f"bank_full{b}") for b in range(2)]
        bank_free = [counter(f"bank_free{b}") for b in range(2)]
        consts_zeroed, consts_ready, gate_slot_zeroed = sem("consts_zeroed"), sem("consts_ready"), sem("gate_slot_zeroed")
        pos_converted, vecs_turned, pos_turned, vecs_ready = sem("pos_converted"), sem("vecs_turned"), sem("pos_turned"), sem("vecs_ready")
        angle_step, sin_ready, half_sin, rope_ready = sem("angle_step"), sem("sin_ready"), sem("half_sin"), sem("rope_ready")
        x_squared, x_rstd_step, x_normed = sem("x_squared"), sem("x_rstd_step"), sem("x_normed")
        x_turned, x_evac = sem("x_turned"), sem("x_evac")
        silu_c_ready, mod_summed, mod_turned, mod_step = sem("silu_c_ready"), sem("mod_summed"), sem("mod_turned"), sem("mod_step")
        x_mod_act, x_mod_dve, h_hi_ready, h_lo_ready = sem("x_mod_act"), sem("x_mod_dve"), sem("h_hi_ready"), sem("h_lo_ready")
        gates_full, gates_out, ident_r_ready = sem("gates_full"), sem("gates_out"), sem("ident_r_ready")
        row_step, row_act, rows_turned, cols_step = sem("row_step"), sem("row_act"), sem("rows_turned"), sem("cols_step")
        head_sinks = counter("head_sinks")
        rope_product, rope_done, v_copied = counter("rope_product"), counter("rope_done"), counter("v_copied")
        q_hi_ready, q_lo_ready = counter("q_hi_ready"), counter("q_lo_ready")
        qk_turned, qk_copied, k_lo_ready = counter("qk_turned"), counter("qk_copied"), counter("k_lo_ready")
        scores_full, max_done, neg_m_done, exp_done = (
            counter("scores_full"), counter("max_done"), counter("neg_m_done"), counter("exp_done"))
        den_step, probs_ready, probs_turned = counter("den_step"), counter("probs_ready"), counter("probs_turned")
        scores_seen, window_merged, prob_t_ready = counter("scores_seen"), counter("window_merged"), counter("prob_t_ready")
        att_full, att_copied, att_gated = counter("att_full"), counter("att_copied"), counter("att_gated")
        y_hi_ready, y_hi_late, y_lo_ready, mix_ready = sem("y_hi_ready"), sem("y_hi_late"), sem("y_lo_ready"), counter("mix_ready")
        head_set, mask_added, dec_ready = counter("head_set"), counter("mask_added"), counter("dec_ready")
        conv_step, conv_silu = counter("conv_step"), counter("conv_silu")
        k_turned, k_weighted, v_ready = counter("k_turned"), counter("k_weighted"), counter("v_ready")
        s_full, s_decayed = counter("s_full"), counter("s_decayed")
        inter_full, inter_ready, intra_full, num_ready = (
            counter("inter_full"), counter("inter_ready"), counter("intra_full"), counter("num_ready"))
        h_den_done, h_rec_done, h_squared = counter("h_den_done"), counter("h_rec_done"), counter("h_squared")
        kv_full, state_ready = counter("kv_full"), counter("state_ready")
        h_norm_step, h_rms_done, h_normed, h_turned = (
            counter("h_norm_step"), counter("h_rms_done"), counter("h_normed"), counter("h_turned"))
        gate_m_done, ym_ready = counter("gate_m_done"), counter("ym_ready")
        gate_sum = counter("gate_sum")
        y2_hi_ready, y2_lo_ready = sem("y2_hi_ready"), sem("y2_lo_ready")
        merged_ready, g_hi_ready, g_lo_ready = (
            counter("merged_ready"), counter("g_hi_ready"), counter("g_lo_ready"))
        gate_bias_added, gate_spread, gate_ready = sem("gate_bias_added"), sem("gate_spread"), sem("gate_ready")

        res_added, res_squared, o_step, o_rms_done, out_ready = (
            sem("res_added"), sem("res_squared"), sem("o_step"), sem("o_rms_done"), sem("out_ready"))

        def unit(phase, per, i, e):
            return e % 2, before(BANK_USES, phase) + per * i + e // 2

        def use(phase, s, n):
            return before(SLOT_USES, phase, s) + n

        def prob_parts(i, m):
            return 15 * i + max(2 * m - 1, 0)

        def window(part):
            return pp[:, 3:5, :].rearrange("p b (a o k) -> p (b a) o k", a=2, o=2)[:, :, part, :]

        def out_parts(n):
            return [slice(0, D)] if n < NB - 1 else [slice(0, HALF), slice(HALF, D)]

        def free(eng, *slots):
            for s in slots:
                eng.nop().then_inc(slot_free[s], 1)

        w_in_v = w_in.rearrange("(k p) c -> p k c", p=P)
        w_att_v = w_att.rearrange("(k p) c -> p k c", p=P)
        w_m_v = w_m.rearrange("(k p) c -> p k c", p=P)
        w_out_v = w_out.rearrange("(k p) c -> p k c", p=P)
        w_ada_v = w_ada.rearrange("(k p) c -> p k c", p=P)
        x_v = x.rearrange("(n p) d -> p n d", p=P)
        out_v = out.rearrange("(n p) d -> p n d", p=P)
        merged_v = merged_dram.rearrange("(k p) t -> p k t", p=P)

        block = ctx.enter_context(nc.Block())

        @block.sync
        def _(sp):
            for n in range(4):
                sp.dma_start(x_in[:, 2 * n:2 * n + 2, :], x_v[:, 2 * n:2 * n + 2, :]).then_inc(x_loaded[n], 16)
            for rows, v, n in ((V_C, c, 8), (V_NW, norm_w, 8), (V_SH, b_ada[0:D], 8), (V_SC, b_ada[D:2 * D], 8),
                               (V_CQ, conv_q, 32), (V_CK, conv_k, 32), (V_MN, m_norm_w, 8)):
                sp.dma_start(vec_rows[rows:rows + n, :], v.rearrange("(r p) -> r p", p=P)).then_inc(vec_loaded, 16)
            sp.dma_start(pos_i[:, :], positions.rearrange("(n p) -> n p", p=P)).then_inc(small_loaded, 16)
            sp.dma_start(freq[:, :], inv_freq[None, :].broadcast_to([P, HD // 2])).then_inc(small_loaded, 16)
            sp.dma_start(sink[:, :], att_sinks[None, :].broadcast_to([P, 16])).then_inc(small_loaded, 16)
            for q in range(2):
                sp.dma_start(bias_if[32 * q:32 * q + 4, :], b_if[4 * q:4 * q + 4, None]).then_inc(small_loaded, 16)
            sp.wait_ge(gate_slot_zeroed, 1)
            sp.dma_start(raw[:, 4, :, 0:4], w_in_v[:, :, MI:MI + 4]).then_inc(slot_loaded[4], 16)
            sp.dma_start(raw[:, 4, :, 32:36], w_in_v[:, :, MF:MF + 4]).then_inc(slot_loaded[4], 16)
            for k in range(KT - 1):
                sp.dma_start(w_mod[:, k, :], w_ada_v[:, k, 0:2 * D]).then_inc(mod_loaded[k], 16)
            for half in range(2):
                t = slice(half * D, (half + 1) * D)
                sp.dma_start(w_mod[:, KT - 1, t], w_ada_v[:, KT - 1, t]).then_inc(mod_loaded[KT - 1 + half], 16)

            def load(src, s, uses):
                after(sp, slot_split[s], uses)
                sp.dma_start(raw[:, s, :, :], src).then_inc(slot_loaded[s], 16)

            with sp.Fori(0, KVH, 1) as i:
                for s in range(2):
                    src = w_in_v[:, :, bass.ds(sp.snap(AQ + s * P + i * 256), P)]
                    load(src, s, use("A", s, 0) + i)
                src_k = w_in_v[:, :, bass.ds(sp.snap(AK + i * HD), HD)]
                src_v = w_in_v[:, :, bass.ds(sp.snap(AV + i * HD), HD)]
                after(sp, slot_split[2], use("A", 2, 0) + i)
                sp.dma_start(raw[:, 2, :, 0:HD], src_k).then_inc(slot_loaded[2], 16)
                sp.dma_start(raw[:, 2, :, HD:P], src_v).then_inc(slot_loaded[2], 16)
                for s in range(3, 5):
                    src = w_in_v[:, :, bass.ds(sp.snap(AZ + (s - 3) * P + i * 256), P)]
                    load(src, s, use("A", s, 0) + i)

            with sp.Fori(0, 4, 1) as i:
                for k in range(2):
                    src = w_in_v[:, :, bass.ds(sp.snap(GA + k * P + i * 256), P)]
                    src_w = w_att_v[:, :, bass.ds(sp.snap(k * P + i * 256), P)]
                    after(sp, slot_split[2 * k + 1], use("B", 2 * k + 1, 0) + i)
                    sp.dma_start(raw[:, 2 * k, :, :], src).then_inc(slot_loaded[2 * k], 16)
                    sp.dma_start(raw[:, 2 * k + 1, :, :], src_w).then_inc(slot_loaded[2 * k + 1], 16)

            with sp.Fori(0, MH, 1) as i:
                for n, (col, s, k) in enumerate(C_LOADS):
                    src = w_in_v[:, :, bass.ds(sp.snap(col + i * MD), P)]
                    load(src, s, use("C", s, k) + 2 * i)
                    if n == C_MASK_AFTER - 1:
                        src = row_pack[bass.ds(sp.snap(i), 1), :].broadcast_to([P, S + NB])
                        after(sp, state_ready, 14 * i)
                        for b in range(2):
                            sp.wait_ge(mix_stored[b], 16 * 5)
                        sp.dma_start(dec[:, :], src).then_inc(dec_loaded, 16)

            with sp.Fori(0, 2, 1) as i:
                for k, s in enumerate(D_SLOTS):
                    src = w_in_v[:, :, bass.ds(sp.snap(GM + k * P + i * 512), P)]
                    load(src, s, use("D1", s, 0) + i)

            with sp.Fori(0, 2, 1) as i:
                for k, s in enumerate(D_SLOTS):
                    src = w_m_v[:, :, bass.ds(sp.snap(k * P + i * 512), P)]
                    load(src, s, use("D2", s, 0) + i)

            sp.wait_ge(gate_bias_added, 1)
            for s in (3, 0, 1, 2):
                load(w_out_v[:, :, s * P:(s + 1) * P], s, use("E", s, 0))
            after(sp, merged_ready, 16)
            sp.dma_start(fin_w[:, :], final_norm_w[None, :].broadcast_to([P, D])).then_inc(fin_loaded, 16)
            for b in range(2):
                after(sp, bank_full[b], before(BANK_USES, "E"))
            for n in range(NB):
                sp.dma_start(res[:, n, :], x_v[:, n, :]).then_inc(res_loaded[n], 16)
            for s in range(4):
                load(w_out_v[:, :, HALF + s * P:HALF + (s + 1) * P], s, use("E2", s, 0))
            for n in range(NB):
                for k, t in enumerate(out_parts(n)):
                    sp.wait_ge(out_ready, n + k + 1)
                    sp.dma_start(out_v[:, n, t], res[:, n, t]).then_inc(out_stored, 16)
            sp.wait_ge(out_stored, 16 * (NB + 1))

        @block.gpsimd
        def _(pool):
            for s, start in counters:
                pool.nop().then_inc(s, start)
            pool.memset(ones[:, :], 1.0).then_inc(consts_zeroed, 1)
            pool.memset(ident[:, :], 0.0).then_inc(consts_zeroed, 1)
            pool.memset(causal[:, :], 0.0).then_inc(consts_zeroed, 1)
            for m in (later, turned_old, turned_new):
                pool.memset(m[:, :], 1.0).then_inc(consts_zeroed, 1)
            pool.memset(neg_col[:, :], NEG).then_inc(consts_zeroed, 1)
            pool.memset(neg_half[:, :], -0.5).then_inc(consts_zeroed, 1)
            pool.memset(raw[:, 4, :, :], 0.0).then_inc(gate_slot_zeroed, 1)
            pool.wait_ge(consts_zeroed, 8)
            pool.affine_select(out=ident[:, :], in_=ident[:, :], compare_op=ALU.not_equal, fill=1.0, base=0,
                               pattern=[[-1, P]], channel_multiplier=1).then_inc(consts_ready, 1)
            for m, fill, base, step in ((causal, NEG, 0, 1), (later, 0.0, -1, 1), (turned_old, 0.0, -1, -1), (turned_new, 0.0, 0, 1)):
                pool.affine_select(out=m[:, :], in_=m[:, :], compare_op=ALU.is_ge, fill=fill, base=base,
                                   pattern=[[step, P]], channel_multiplier=-step).then_inc(consts_ready, 1)

            for n in range(NB):
                pool.wait_ge(x_squared, n + 1)
                pool.tensor_scalar(x_ssq[:, n:n + 1], x_ssq[:, n:n + 1], 1.0 / D, EPS, ALU.mult, ALU.add).then_inc(x_rstd_step, 1)
                pool.wait_ge(x_rstd_step, 2 * n + 1)
                pool.tensor_tensor(x_rstd[:, n:n + 1], x_ssq[:, n:n + 1], neg_half[:, n:n + 1], ALU.pow).then_inc(x_rstd_step, 1)

            one = ones[:, 0:1, None].broadcast_to([P, KT, P])

            def split(s, uses, loads, hi=None, lo=None):
                if hi is None:
                    after(pool, slot_free[s], uses)
                hi = w_hi[:, s, :, :] if hi is None else hi
                lo = w_lo[:, s, :, :] if lo is None else lo
                pool.wait_ge(slot_loaded[s], 16 * loads)
                pool.tensor_tensor(hi, raw[:, s, :, :], one, ALU.mult).then_inc(slot_hi[s], 1)
                after(pool, slot_hi[s], uses + 1)
                pool.tensor_tensor(lo, raw[:, s, :, :], hi.bitcast(F32), ALU.subtract).then_inc(slot_split[s], 1)

            def loads(phase, s, n):
                return before(SLOT_DMAS, phase, s) + n

            split(4, use("G", 4, 0), loads("G", 4, 2))
            with pool.Fori(0, KVH, 1) as i:
                for s in range(5):
                    per = 2 if s == 2 else 1
                    split(s, use("A", s, 0) + i, loads("A", s, per) + per * i)
            for s in range(4):
                split(s, use("B", s, 0), loads("B", s, 1))
            after(pool, att_gated, 2 * KVH)
            for k in range(KT):
                pool.tensor_tensor(y_hi[:, k, HALF:S], y[:, k, HALF:S], ones[:, 0:1].broadcast_to([P, HALF]), ALU.mult).then_inc(y_hi_late, 1)
            with pool.Fori(0, 3, 1) as i:
                for s in range(4):
                    split(s, use("B", s, 1) + i, loads("B", s, 2) + i)
            with pool.Fori(0, MH, 1) as i:
                for n, (_, s, k) in enumerate(C_LOADS):
                    split(s, use("C", s, k) + 2 * i, loads("C", s, k + 1) + 2 * i)
                    if n == C_MASK_AFTER - 1:
                        pool.wait_ge(dec_loaded, 16 * (i + 1))
                        d = dec[:, 0:S].rearrange("p (n t) -> p n t", n=NB)
                        pool.tensor_tensor(d, d, causal[:, None, :].broadcast_to([P, NB, P]), ALU.add).then_inc(mask_added, 1)
            for phase in ("D1", "D2"):
                with pool.Fori(0, 2, 1) as i:
                    for s in D_SLOTS:
                        split(s, use(phase, s, 0) + i, loads(phase, s, 1) + i)
            for s in (3, 0, 1, 2):
                split(s, use("E", s, 0), loads("E", s, 1))
            for b in range(2):
                after(pool, bank_full[b], before(BANK_USES, "E"))
            for s in range(4):
                split(s, use("E2", s, 0), loads("E2", s, 1), hi=w2_hi[:, s, :, :], lo=w2_lo[:, s, :, :])

        @block.tensor
        def _(pe):
            def passes(o, lhs, rhs, k, first, last):
                (lh, ll), (rh, rl) = lhs, rhs
                pe.matmul(o, lh, rh, start=first, stop=False)
                pe.matmul(o, lh, rl, start=False, stop=False)
                return pe.matmul(o, ll, rh, start=False, stop=last)

            def feature_unit(phase, per, i, e, s, half, src_hi, src_lo, ready=None):
                b, n = unit(phase, per, i, e)
                after(pe, bank_free[b], n)
                t = slice(half * HALF, (half + 1) * HALF)
                for k in range(KT):
                    if ready is not None:
                        pe.wait_ge(ready, half * KT + k + 1)
                    ins = passes(bank(b), (w_hi[:, s, k, :], w_lo[:, s, k, :]),
                                 (src_hi[:, k, t], src_lo[:, k, t]), k, k == 0, k == KT - 1)
                ins.then_inc(bank_full[b], 1)

            def token_unit(phase, per, i, e, blk, wh, wl, n_slots):
                b, n = unit(phase, per, i, e)
                after(pe, bank_free[b], n)
                t = slice(blk * P, (blk + 1) * P)
                o = bank(b)[:, 0:n_slots * P].rearrange("p (s c) -> p s c", s=n_slots)
                for k in range(KT):
                    ins = passes(o, (h_hi[:, k, t], h_lo[:, k, t]), (wh[:, :, k, :], wl[:, :, k, :]), k, k == 0, k == KT - 1)
                ins.then_inc(bank_full[b], 1)

            pe.wait_ge(consts_ready, 1)
            pe.wait_ge(vec_loaded, 16 * 7)
            pe.transpose(bank(2)[:, 0:V_N], vec_rows[:, :], ident[0:V_N, 0:V_N]).then_inc(vecs_turned, 1)
            pe.wait_ge(pos_converted, 1)
            pe.transpose(bank(3)[:, 0:NB], pos_f[:, :], ident[0:NB, 0:NB]).then_inc(pos_turned, 1)
            for q in range(16):
                half, k = q // 8, q % 8
                b = 4 + q % 4
                if k == 0:
                    pe.wait_ge(x_normed, 4 * half + 4)
                if q >= 4:
                    pe.wait_ge(x_evac, q - 3)
                for n in range(4):
                    ins = pe.transpose(bank(b)[:, n * P:(n + 1) * P], x_in[:, 4 * half + n, k * P:(k + 1) * P], ident[:, :])
                ins.then_inc(x_turned, 1)
            pe.wait_ge(x_evac, 16)
            for f in range(16):
                if f % 8 == 0:
                    pe.wait_ge(mod_summed, KT + f // 8)
                ins = pe.transpose(bank(2 + f // 4)[:, (f % 4) * P:(f % 4 + 1) * P], mod_acc[:, f * P:(f + 1) * P], ident[:, :])
                if f % 8 == 7:
                    ins.then_inc(mod_turned, 1)

            after(pe, slot_split[4], use("G", 4, 1))
            for k in range(KT):
                pe.wait_ge(h_lo_ready, k + 1)
                for half in range(2):
                    t = slice(half * HALF, (half + 1) * HALF)
                    ins = passes(bank(6 + half), (w_hi[:, 4, k, :], w_lo[:, 4, k, :]), (h_hi[:, k, t], h_lo[:, k, t]),
                                 k, k == 0, k == KT - 1)
            ins.then_inc(gates_full, 1)


            def turn_k(i, m):
                after(pe, rope_done, 2 * (NB * i + m + 1))
                after(pe, k_lo_ready, NB * i + m)
                pe.transpose(bank(6)[:, 0:P], roped[:, m % 2, 4:6, :, :], ident[:, :])

            def turn_q(i, m):
                after(pe, q_lo_ready, NB * i + m + 1)
                after(pe, qk_copied, 2 * (NB * i + m))
                for g in range(4):
                    ins = pe.matmul(bank(2)[:, g * P:(g + 1) * P], q_parts[:, m % 2, g, :, :], ident_r[:, :], start=True, stop=True)
                ins.then_inc(qk_turned, 1)

            def scores(i, m):
                after(pe, qk_copied, 2 * (NB * i + m + 1))
                after(pe, k_lo_ready, NB * i + m + 1)
                after(pe, exp_done, 5 * (NB * i + m))
                k0 = P if m == 0 else 0
                keys = slice(max(m - 1, 0) * P, (m + 1) * P)
                for odd in range(2):
                    for pair in range(2):
                        o = bank(3 + odd)[:, pair * 2 * P + k0:(pair + 1) * 2 * P]
                        q = q_t[:, 2 * pair + odd, :]
                        pe.matmul(o, q, k_hi[:, keys], start=True, stop=False)
                        ins = pe.matmul(o, q, k_lo[:, keys], start=False, stop=True)
                ins.then_inc(scores_full, 1)

            def turn_probs(i, m):
                after(pe, prob_t_ready, prob_parts(i, m))
                for g in range(4):
                    after(pe, probs_ready, 4 * (NB * i + m) + g + 1)
                    ins = pe.transpose(bank(5)[:, g * P:(g + 1) * P], prob[:, g, :], ident[:, :])
                ins.then_inc(probs_turned, 1)

            def weigh_v(i, m):
                after(pe, prob_t_ready, prob_parts(i, m + 1))
                after(pe, v_copied, NB * i + m + 1)
                after(pe, att_copied, NB * i + m)
                for odd in range(2):
                    for old in range(1 if m == 0 else 0, 2):
                        ins = pe.matmul(pp[odd * HD:(odd + 1) * HD, 7, 0:2 * P], v_tok[:, m - 1 + old, :],
                                        prob_t[:, old, odd * 2 * P:(odd + 1) * 2 * P],
                                        start=(old == (1 if m == 0 else 0)), stop=(old == 1), skip_group_check=True)
                ins.then_inc(att_full, 1)

            def attend(i, before_head=None):
                for u in range(12):
                    if u < NB:
                        if u == 0:
                            for s in range(3):
                                after(pe, slot_split[s], use("A", s, 1) + i)
                        token_unit("A", 6, i, u, u, w_hi[:, 0:3], w_lo[:, 0:3], 3)
                    else:
                        s = 3 + (u - NB) // 2
                        if u % 2 == 0:
                            after(pe, slot_split[s], use("A", s, 1) + i)
                        feature_unit("A", 6, i, u, s, u % 2, h_hi, h_lo)
                    if u == 0 and before_head is not None:
                        weigh_v(before_head, NB - 1)
                    if u == 2:
                        pe.wait_ge(gates_out, 4)
                        pe.wait_ge(ident_r_ready, 1)
                    if 2 <= u <= NB + 1:
                        turn_k(i, u - 2)
                    if 5 <= u:
                        weigh_v(i, u - 5)
                    if 2 <= u <= NB + 1:
                        turn_q(i, u - 2)
                    if 4 <= u <= NB + 3:
                        turn_probs(i, u - 4)
                    if 3 <= u <= NB + 2:
                        scores(i, u - 3)

            attend(0)
            with pe.Fori(0, KVH - 1, 1) as i:
                attend(i + 1, i)
            pe.wait_ge(row_act, 5)
            after(pe, qk_copied, 2 * NB * KVH)
            after(pe, exp_done, 5 * NB * KVH)
            for n in range(NB):
                ins = pe.transpose(bank(2 + n // 4)[:, (n % 4) * P:(n % 4 + 1) * P], row_all[:, n * P:(n + 1) * P], ident[:, :])
            ins.then_inc(rows_turned, 1)
            weigh_v(KVH - 1, NB - 1)

            with pe.Fori(0, 4, 1) as i:
                for k in range(2):
                    after(pe, slot_split[2 * k], use("B", 2 * k, 1) + i)
                    for half in range(2):
                        feature_unit("B", 4, i, 4 * k + half, 2 * k, half, h_hi, h_lo)
                    after(pe, slot_split[2 * k + 1], use("B", 2 * k + 1, 1) + i)
                    for half in range(2):
                        feature_unit("B", 4, i, 4 * k + 2 + half, 2 * k + 1, half, y_hi, y_lo, ready=y_lo_ready)

            def turn_k(i, n):
                if n == 0:
                    after(pe, conv_silu, 4 * (i + 1))
                    after(pe, ym_ready, 4 * i)
                    pe.wait_ge(cols_step, 3)
                else:
                    after(pe, k_weighted, NB * i + n)
                for f in range(2):
                    ins = pe.transpose(bank(2)[:, f * P:(f + 1) * P], mk_t[:, f, n * P:(n + 1) * P], ident[:, :])
                ins.then_inc(k_turned, 1)

            def key_query(i, n):
                after(pe, s_decayed, NB * i + n)
                for f in range(2):
                    t = slice(n * P, (n + 1) * P)
                    ins = pe.matmul(bank(3)[:, 0:P], mk_t[:, f, t], mq_t[:, f, t], start=(f == 0), stop=(f == 1))
                ins.then_inc(s_full, 1)

            def chunk(i, n):
                if n:
                    after(pe, state_ready, 14 * i + 2 * n)
                    after(pe, inter_ready, 7 * i + n - 1 if n > 1 else 7 * i)
                    for f in range(2):
                        ins = pe.matmul(bank(4)[:, 0:MV], mq_t[:, f, n * P:(n + 1) * P], state[:, f, :], start=(f == 0), stop=(f == 1))
                    ins.then_inc(inter_full, 1)
                after(pe, s_decayed, NB * i + n + 1)
                after(pe, v_ready, NB * i + n + 1)
                after(pe, num_ready, NB * i + n)
                pe.matmul(bank(5)[:, 0:MV], s_dec[:, n % 2, :], v_aug[:, n % 2, :], start=True, stop=True).then_inc(intra_full, 1)
                if n < NB - 1:
                    after(pe, k_weighted, NB * i + n + 1)
                    after(pe, state_ready, 14 * i + 2 * n)
                    for f in range(2):
                        ins = pe.matmul(bank(6 + f)[:, 0:MV], k_w[:, n % 2, f * P:(f + 1) * P], v_aug[:, n % 2, :], start=True, stop=True)
                    ins.then_inc(kv_full, 1)

            with pe.Fori(0, MH, 1) as i:
                for e, (kind, n) in enumerate(C_UNITS):
                    if kind == "mv":
                        if n == 0:
                            for s in range(2):
                                after(pe, slot_split[s], use("C", s, 2) + 2 * i)
                        token_unit("C", 12, i, e, n, w_hi[:, 0:2], w_lo[:, 0:2], 2)
                        turn_k(i, n)
                        key_query(i, n)
                    else:
                        s, k = C_SLOT[f"{kind}{n // 2}"]
                        if n % 2 == 0:
                            after(pe, slot_split[s], use("C", s, k + 1) + 2 * i)
                        feature_unit("C", 12, i, e, s, n % 2, h_hi, h_lo)
                    if kind == "mv" and n >= 1:
                        chunk(i, n - 1)
                    if (kind, n) == ("mo", 0):
                        chunk(i, NB - 1)
                    if (kind, n) == ("mo", 2):
                        after(pe, k_weighted, NB * (i + 1))
                        for q in range(4):
                            f, half = q // 2, q % 2
                            after(pe, h_normed, NB * i + 4 * half + 4)
                            for m in range(4):
                                ins = pe.transpose(bank(2 + q)[:, m * P:(m + 1) * P], num[:, 4 * half + m, f * P:(f + 1) * P], ident[:, :])
                            ins.then_inc(h_turned, 1)

            for phase, hi, lo, ready in (("D1", h_hi, h_lo, None), ("D2", y2_hi, y_lo, y2_lo_ready)):
                with pe.Fori(0, 2, 1) as i:
                    for k, s in enumerate(D_SLOTS):
                        after(pe, slot_split[s], use(phase, s, 1) + i)
                        for half in range(2):
                            feature_unit(phase, 4, i, 2 * k + half, s, half, hi, lo, ready=ready)

            pe.wait_ge(gate_bias_added, 1)
            for half in range(2):
                ins = pe.matmul(bank(6 + half), ones[:, :], gate_acc[:, half * HALF:(half + 1) * HALF], start=True, stop=True)
            ins.then_inc(gate_spread, 1)
            for half in range(2):
                for s in range(4):
                    if half == 0:
                        after(pe, slot_split[s], use("E", s, 1))
                    else:
                        after(pe, slot_split[s], use("E2", s, 1))
                wh, wl = (w_hi[:, 0:4], w_lo[:, 0:4]) if half == 0 else (w2_hi[:, :], w2_lo[:, :])
                for n in range(NB):
                    if half == 0:
                        after(pe, g_lo_ready, 15 if n < NB // 2 else 16)
                    b, uses = unit("E", 8, 0, half * NB + n)
                    after(pe, bank_free[b], uses)
                    o = bank(b).rearrange("p (s c) -> p s c", s=4)
                    t = slice(n * P, (n + 1) * P)
                    for k in range(KT):
                        ins = passes(o, (g_hi[:, k, t], g_lo[:, k, t]), (wh[:, :, k, :], wl[:, :, k, :]), k, k == 0, k == KT - 1)
                    ins.then_inc(bank_full[b], 1)

        @block.scalar
        def _(act):
            def full(phase, per, i, e):
                b, n = unit(phase, per, i, e)
                after(act, bank_full[b], n + 1)
                return b

            junk = pp[:, 0:2, :].rearrange("p b c -> p (b c)")
            for n in range(NB):
                act.wait_ge(x_loaded[n // 2], 16)
                if n:
                    act.wait_ge(x_squared, n)
                act.activation(junk, x_in[:, n, :], ACT.Square, accum_out=x_ssq[:, n:n + 1]).then_inc(x_squared, 1)
            act.wait_ge(vecs_ready, 1)
            act.activation(silu_c[:, :], vecs[:, V_C:V_C + KT], ACT.Silu).then_inc(silu_c_ready, 1)
            for q in range(16):
                act.wait_ge(x_turned, q + 1)
                act.activation(xnt[:, q % 8, q // 8 * HALF:(q // 8 + 1) * HALF], bank(4 + q % 4), ACT.Copy).then_inc(x_evac, 1)
            act.wait_ge(angle_step, 9)
            act.activation(sin[:, :, :], ang[:, :, :], ACT.Sin).then_inc(sin_ready, 1)
            act.activation(turns[:, :, :], ang[:, :, :], ACT.Sin, scale=0.5).then_inc(half_sin, 1)
            act.wait_ge(mod_step, 5)
            act.wait_ge(x_evac, 16)
            for k in range(KT):
                act.activation(h_hi[:, k, :], xnt[:, k, :], ACT.Identity, scale=scale1[:, k:k + 1], bias=shift[:, k:k + 1]).then_inc(h_hi_ready, 1)
                if k in MOD_BY_ACT:
                    act.activation(x_mod[:, k, :], xnt[:, k, :], ACT.Identity, scale=scale1[:, k:k + 1], bias=shift[:, k:k + 1]).then_inc(x_mod_act, 1)

            act.wait_ge(h_lo_ready, KT)
            act.activation(ident_r[:, :], ident[:, :], ACT.Copy).then_inc(ident_r_ready, 1)

            def gate_row_step(n):
                if n == 0:
                    act.wait_ge(row_step, 1)
                    act.activation(row_e[32:36, :], row_e[32:36, :], ACT.Exp).then_inc(row_act, 1)
                    act.wait_ge(row_act, 1)
                    act.activation(row_e[32:36, :], row_e[32:36, :], ACT.Ln, bias=1.0).then_inc(row_act, 1)
                if n == 12:
                    act.wait_ge(row_step, 13)
                    act.activation(row_all[96:100, :], row_m[0:4, :], ACT.Exp, scale=-1.0).then_inc(row_act, 1)
                    act.activation(row_all[64:68, :], row_all[64:68, :], ACT.Exp).then_inc(row_act, 1)
                    act.activation(row_all[32:36, :], row_all[32:36, :], ACT.Exp).then_inc(row_act, 1)
                    act.wait_ge(row_act, 5)
                    act.dma_start(row_pack[:, 0:S], row_c[0:4, :]).then_inc(row_stored, 16)
                    act.dma_start(row_pack[:, S:S + NB], row_all[32:36, P - 1:S:P],
                                  allow_slow_non_contiguous=True).then_inc(row_stored, 16)

            def q_high(i, m):
                after(act, rope_done, 2 * (NB * i + m + 1))
                if m >= 2:
                    after(act, qk_turned, NB * i + m - 1)
                act.activation(q_parts[:, m % 2, :, 0, :], roped[:, m % 2, 0:4, :, :].rearrange("p h a d -> p h (a d)"), ACT.Copy).then_inc(q_hi_ready, 1)

            def copy_qk(i, m):
                after(act, qk_turned, NB * i + m + 1)
                after(act, scores_full, NB * i + m)
                act.activation(q_t[:, :, :], bank(2).rearrange("p (g t) -> p g t", g=4), ACT.Copy).then_inc(qk_copied, 1)
                act.activation(k_hi[:, m * P:(m + 1) * P], bank(6)[:, 0:P], ACT.Copy).then_inc(qk_copied, 1)

            def exponentials(i, m):
                after(act, neg_m_done, 2 * (NB * i + m + 1))
                after(act, probs_turned, NB * i + m)
                for g in range(4):
                    act.activation(prob[:, g, :], window(1)[:, g, :], ACT.Exp, bias=neg_m[:, g:g + 1], scale=ATT_SCALE,
                                   accum_out=p_sum[:, g:g + 1]).then_inc(exp_done, 1)
                act.activation(sink_e[:, :], sink_d[:, :], ACT.Exp).then_inc(exp_done, 1)

            def copy_att(i, m):
                after(act, att_full, NB * i + m + 1)
                dst = y[:, bass.ds(2 * i, 2), m * P:(m + 1) * P]
                act.activation(dst, bank(7)[:, 0:2 * P].rearrange("p (a t) -> p a t", a=2), ACT.Copy).then_inc(att_copied, 1)

            def attend(i, first):
                for u in range(14):
                    if 3 <= u <= NB + 2:
                        copy_qk(i, u - 3)
                    if 6 <= u:
                        if u == 6 and not first:
                            act.wait_ge(row_stored, 32)
                        copy_att(i, u - 6)
                    if 4 <= u <= NB + 3:
                        exponentials(i, u - 4)
                    if 1 <= u <= NB:
                        q_high(i, u - 1)
                    if 9 <= u <= 12:
                        e = u - 1
                        b = full("A", 6, i, e)
                        if e % 2:
                            free(act, 3 + (e - NB) // 2)
                        after(act, att_gated, 2 * i)
                        half = e % 2
                        act.activation(silu_az[:, (e - NB) // 2, half * HALF:(half + 1) * HALF], bank(b), ACT.Silu).then_inc(bank_free[b], 1)
                    if first:
                        gate_row_step(u)

            attend(0, True)
            with act.Fori(1, KVH, 1) as i:
                attend(i, False)

            after(act, att_gated, 2 * KVH - 1)
            for k in range(KT):
                act.activation(y_hi[:, k, 0:HALF], y[:, k, 0:HALF], ACT.Copy).then_inc(y_hi_ready, 1)
            with act.Fori(0, 4, 1) as i:
                for k in range(2):
                    for half in range(2):
                        b = full("B", 4, i, 4 * k + half)
                        if half:
                            free(act, 2 * k)
                        after(act, mix_ready, 4 * i + 2 * k)
                        act.activation(sig_a[:, half, :], bank(b), ACT.Sigmoid).then_inc(bank_free[b], 1)
                    dst = merged_v[:, bass.ds(2 * i + k, 1), :]
                    after(act, mix_ready, 4 * i + 2 * k + 2)
                    act.dma_start(dst, mix_a[:, k:k + 1, :]).then_inc(mix_stored[k], 16)

            def conv_out(i, kind, n):
                after(act, conv_step, 4 * (4 * i + n // 2 + (2 if kind == "mk" else 0) + 1))
                act.activation((mk_t if kind == "mk" else mq_t)[:, n // 2, :], conv[:, :], ACT.Silu).then_inc(conv_silu, 1)

            def decays(first, last):
                for m in range(first, last):
                    act.activation(dec[:, m * P:(m + 1) * P], dec[:, m * P:(m + 1) * P], ACT.Exp,
                                   bias=h_cols[:, m, 0:1]).then_inc(dec_ready, 1)

            with act.Fori(0, MH, 1) as i:
                after(act, head_set, i + 1)
                for e, (kind, n) in enumerate(C_UNITS):
                    b = full("C", 12, i, e)
                    if kind == "mv" and n == NB - 1:
                        free(act, 0, 1)
                    if kind != "mv" and n % 2:
                        free(act, C_SLOT[f"{kind}{n // 2}"][0])
                    cols_half = slice((n % 2) * HALF, (n % 2 + 1) * HALF)
                    if kind in ("mq", "mk"):
                        f = n // 2 + (2 if kind == "mk" else 0)
                        if n % 2 == 0:
                            after(act, conv_step, 4 * (4 * i + f))
                            after(act, h_turned, 4 * i)
                        act.activation(xpad[:, CW - 1 + (n % 2) * HALF:CW - 1 + (n % 2 + 1) * HALF], bank(b), ACT.Copy).then_inc(bank_free[b], 1)
                        if n % 2 and (kind, n) != ("mk", 3):
                            conv_out(i, kind, n)
                    if kind == "mv":
                        if n >= 2:
                            after(act, intra_full, NB * i + n - 1)
                            after(act, kv_full, 7 * i + n - 1)
                        act.activation(v_aug[:, n % 2, 0:MD], bank(b)[:, 0:MD], ACT.Copy).then_inc(v_ready, 1)
                        after(act, v_ready, NB * i + n + 1)
                        after(act, k_turned, NB * i + n + 1)
                        act.activation(k_w[:, n % 2, :], bank(2)[:, 0:MD], ACT.Copy, scale=h_cols[:, n, 2:3]).then_inc(k_weighted, 1)
                        act.nop().then_inc(bank_free[b], 1)
                        if n == 0:
                            decays(2, NB)
                    if kind == "mz":
                        after(act, ym_ready, 4 * i)
                        act.activation(gate_m[:, n // 2, cols_half], bank(b), ACT.Silu).then_inc(bank_free[b], 1)
                        if n == 0:
                            conv_out(i, "mk", 3)
                            after(act, mask_added, i + 1)
                            decays(0, 2)
                    if kind == "mo":
                        after(act, gate_m_done, 4 * i + n)
                        act.activation(sig_o[:, :], bank(b), ACT.Sigmoid).then_inc(bank_free[b], 1)
                    m = n - 1 if kind == "mv" else NB - 1
                    if (kind == "mv" and n >= 1) or (kind, n) == ("mo", 0):
                        if m:
                            after(act, inter_full, 7 * i + m)
                            after(act, h_squared, NB * i + m)
                            after(act, num_ready, NB * i + m)
                            act.activation(inter[:, :], bank(4)[:, 0:MV], ACT.Copy, scale=h_cols[:, m, 1:2]).then_inc(inter_ready, 1)
                        after(act, h_rec_done, NB * i + m + 1)
                        act.activation(inter[:, 0:MD], num[:, m, 0:MD], ACT.Square, scale=h_rec[:, m:m + 1],
                                       accum_out=h_ssq[:, m:m + 1]).then_inc(h_squared, 1)
                    if (kind, n) == ("mo", 0):
                        after(act, h_norm_step, 3 * i + 1)
                        act.activation(h_rms[:, :], h_ms[:, :], ACT.Sqrt).then_inc(h_rms_done, 1)

            after(act, ym_ready, 4 * MH)
            act.dma_start(gate_row[0:1, :], b_ada[None, 2 * D:3 * D]).then_inc(gate_row_loaded, 16)
            with act.Fori(0, 2, 1) as i:
                for s in range(4):
                    src = w_ada_v[:, bass.ds(4 * i + s, 1), 2 * D:3 * D]
                    after(act, gate_sum, 4 * i + s - 1 if s >= 1 else 4 * i)
                    act.dma_start(w_gate[:, s % 2:s % 2 + 1, :], src).then_inc(w_gate_loaded[s % 2], 16)
                    for half in range(2):
                        b = full("D1", 4, i, 2 * s + half)
                        if half:
                            free(act, D_SLOTS[s])
                        dst = sig_m[:, bass.ds(4 * i + s, 1), half * HALF:(half + 1) * HALF]
                        act.activation(dst, bank(b)[:, None, :], ACT.Sigmoid).then_inc(bank_free[b], 1)
            for b in range(2):
                after(act, bank_full[b], before(BANK_USES, "D2"))
            for half in range(2):
                t = slice(half * HALF, (half + 1) * HALF)
                for k in range(KT):
                    act.activation(y2_hi[:, k, t], y[:, k, t], ACT.Copy).then_inc(y2_hi_ready, 1)
            act.wait_ge(gate_bias_added, 1)

            def load_mix(i, s):
                src = merged_v[:, bass.ds(4 * i + s, 1), :]
                act.dma_start(mix_in[:, s % 2:s % 2 + 1, :], src).then_inc(mix_loaded[s % 2], 16)

            with act.Fori(0, 2, 1) as i:
                load_mix(i, 0)
                for s in range(4):
                    for half in range(2):
                        if half and s < 3:
                            load_mix(i, s + 1)
                        n = 8 * i + 2 * s + half
                        after(act, merged_ready, n + 1)
                        dst = g_hi[:, bass.ds(4 * i + s, 1), half * HALF:(half + 1) * HALF]
                        act.activation(dst, merged[:, None, :], ACT.Copy).then_inc(g_hi_ready, 1)

            for half in range(2):
                for n in range(NB):
                    e = half * NB + n
                    act.wait_ge(res_added, e + 1)
                    if e:
                        act.wait_ge(res_squared, e)
                    act.activation(bank(2), res[:, n, half * HALF:(half + 1) * HALF], ACT.Square,
                                   accum_out=o_ssq[:, n, half:half + 1]).then_inc(res_squared, 1)
                    if half:
                        act.wait_ge(o_step, 3 * n + 2)
                        act.activation(o_rms[:, n:n + 1], o_ms[:, n:n + 1], ACT.Sqrt).then_inc(o_rms_done, 1)

        @block.vector
        def _(dve):
            def full(phase, per, i, e):
                b, n = unit(phase, per, i, e)
                after(dve, bank_full[b], n + 1)
                return b

            for n in range(NB):
                dve.wait_ge(x_rstd_step, 2 * n + 2)
                dve.tensor_scalar(x_in[:, n, :], x_in[:, n, :], x_rstd[:, n:n + 1], None, ALU.mult).then_inc(x_normed, 1)
            dve.wait_ge(small_loaded, 16 * 5)
            dve.tensor_copy(pos_f[:, :], pos_i[:, :]).then_inc(pos_converted, 1)
            dve.tensor_scalar(neg_sink[:, :], sink[:, :], -1.0, None, ALU.mult).then_inc(angle_step, 1)
            dve.wait_ge(vecs_turned, 1)
            dve.tensor_copy(vecs[:, :], bank(2)[:, 0:V_N]).then_inc(vecs_ready, 1)
            dve.wait_ge(pos_turned, 1)
            dve.tensor_copy(pos_col[:, :], bank(3)[:, 0:NB]).then_inc(angle_step, 1)
            dve.wait_ge(angle_step, 2)
            shape = [P, NB, HD // 2]

            def angle_step_of(k):
                if k == 0:
                    dve.tensor_tensor(ang[:, :, :], pos_col[:, :, None].broadcast_to(shape), freq[:, None, :].broadcast_to(shape),
                                      ALU.mult).then_inc(angle_step, 1)
                elif k == 1:
                    dve.wait_ge(angle_step, 3)
                    dve.tensor_scalar(turns[:, :, :], ang[:, :, :], 1.0 / TWO_PI, None, ALU.mult).then_inc(angle_step, 1)
                elif k == 2:
                    dve.wait_ge(angle_step, 4)
                    dve.tensor_copy(turns_i[:, :, :], turns[:, :, :]).then_inc(rope_ready, 1)
                elif k == 3:
                    dve.wait_ge(rope_ready, 1)
                    dve.tensor_copy(turns[:, :, :], turns_i[:, :, :]).then_inc(rope_ready, 1)
                elif k < 8:
                    dve.wait_ge(rope_ready, 2)
                    dve.wait_ge(angle_step, k)
                    dve.scalar_tensor_tensor(out=ang[:, :, :], in0=turns[:, :, :], scalar=-(PI_A, PI_B, PI_C1, PI_C2)[k - 4],
                                             in1=ang[:, :, :], op0=ALU.mult, op1=ALU.add).then_inc(angle_step, 1)
                else:
                    dve.wait_ge(angle_step, 8)
                    dve.tensor_scalar(ang[:, :, :], ang[:, :, :], PI_TOP, -PI_TOP, ALU.min, ALU.max).then_inc(angle_step, 1)

            dve.wait_ge(silu_c_ready, 1)
            for k in range(KT):
                for half in range(2 if k == KT - 1 else 1):
                    t = slice(half * D, (half + 1) * D) if k == KT - 1 else slice(0, 2 * D)
                    dve.wait_ge(mod_loaded[k + half], 16)
                    if k == 0:
                        dve.tensor_scalar(mod_acc[:, :], w_mod[:, 0, :], silu_c[:, 0:1], None, ALU.mult).then_inc(mod_summed, 1)
                    else:
                        dve.wait_ge(mod_summed, k)
                        dve.scalar_tensor_tensor(out=mod_acc[:, t], in0=w_mod[:, k, t], scalar=silu_c[:, k:k + 1], in1=mod_acc[:, t],
                                                 op0=ALU.mult, op1=ALU.add).then_inc(mod_summed, 1)
                angle_step_of(k)
            angle_step_of(KT)
            for half in range(2):
                dve.wait_ge(mod_turned, half + 1)
                dve.tensor_reduce(mod_col[:, half * KT:(half + 1) * KT],
                                  pp[:, 2 + 2 * half:4 + 2 * half, :].rearrange("p b (a t) -> p (b a) t", a=4), AX.X, ALU.add).then_inc(mod_step, 1)
            dve.wait_ge(mod_step, 2)
            dve.tensor_tensor(scale_t[:, :], mod_col[:, KT:2 * KT], vecs[:, V_SC:V_SC + KT], ALU.add).then_inc(mod_step, 1)
            dve.tensor_tensor(shift[:, :], mod_col[:, 0:KT], vecs[:, V_SH:V_SH + KT], ALU.add).then_inc(mod_step, 1)
            dve.wait_ge(mod_step, 4)
            dve.scalar_tensor_tensor(out=scale1[:, :], in0=scale_t[:, :], scalar=1.0, in1=vecs[:, V_NW:V_NW + KT],
                                     op0=ALU.add, op1=ALU.mult).then_inc(mod_step, 1)
            dve.wait_ge(mod_step, 5)
            dve.wait_ge(consts_ready, 5)
            dve.wait_ge(x_evac, 16)
            for k in range(-1, KT):
                if k + 1 < KT and k + 1 not in MOD_BY_ACT:
                    dve.tensor_scalar(x_mod[:, k + 1, :], xnt[:, k + 1, :], scale1[:, k + 1:k + 2], shift[:, k + 1:k + 2],
                                      ALU.mult, ALU.add).then_inc(x_mod_dve, 1)
                if k >= 0:
                    dve.wait_ge(h_hi_ready, k + 1)
                    by_act = sum(m in MOD_BY_ACT for m in range(k + 1))
                    if k in MOD_BY_ACT:
                        dve.wait_ge(x_mod_act, by_act)
                    else:
                        dve.wait_ge(x_mod_dve, k + 1 - by_act)
                    dve.tensor_tensor(h_lo[:, k, :], x_mod[:, k, :], h_hi[:, k, :].bitcast(F32), ALU.subtract).then_inc(h_lo_ready, 1)

            dve.wait_ge(half_sin, 1)
            dve.tensor_tensor(turns[:, :, :], turns[:, :, :], turns[:, :, :], ALU.mult).then_inc(rope_ready, 1)
            dve.wait_ge(rope_ready, 3)
            dve.tensor_scalar(cos[:, :, :], turns[:, :, :], -2.0, 1.0, ALU.mult, ALU.add).then_inc(rope_ready, 1)

            def gate_row_step(n):
                if n == 0:
                    dve.wait_ge(gates_full, 1)
                    free(dve, 4)
                    for half in range(2):
                        t = slice(half * HALF, (half + 1) * HALF)
                        for p0 in (0, 32):
                            dve.tensor_scalar(row_if[p0:p0 + 4, t], bank(6 + half)[p0:p0 + 4, :], bias_if[p0:p0 + 4, :],
                                              None, ALU.add).then_inc(gates_out, 1)
                    dve.wait_ge(gates_out, 4)
                    dve.scalar_tensor_tensor(out=row_e[32:36, :], in0=row_if[32:36, :], scalar=-1.0, in1=row_if[32:36, :],
                                             op0=ALU.mult, op1=ALU.min).then_inc(row_step, 1)
                if n == 1:
                    dve.memset(row_all[:, :], 0.0).then_inc(row_step, 1)
                    dve.memset(row_keep[0:4, :], 1.0).then_inc(row_step, 1)
                if n == 2:
                    dve.wait_ge(row_step, 3)
                    dve.memset(row_keep[0:4, 0:S:P], 0.0).then_inc(row_step, 1)
                    dve.memset(m_prev[:, :], 0.0).then_inc(row_step, 1)
                if n == 9:
                    dve.wait_ge(row_act, 2)
                    dve.scalar_tensor_tensor(out=row_logf[0:4, :], in0=row_if[32:36, :], scalar=0.0, in1=row_e[32:36, :],
                                             op0=ALU.min, op1=ALU.subtract).then_inc(row_step, 1)
                    dve.wait_ge(row_step, 6)
                    dve.tensor_tensor_scan(out=row_b[0:4, :], data0=row_keep[0:4, :], data1=row_logf[0:4, :], initial=0.0,
                                           op0=ALU.mult, op1=ALU.add).then_inc(row_step, 1)
                if n == 10:
                    dve.tensor_tensor_scan(out=row_m[0:4, :], data0=row_logf[0:4, :], data1=row_if[0:4, :], initial=0.0,
                                           op0=ALU.add, op1=ALU.max).then_inc(row_step, 1)
                if n == 11:
                    dve.wait_ge(row_step, 7)
                    dve.tensor_tensor(row_all[0:4, :], row_if[0:4, :], row_b[0:4, :], ALU.subtract).then_inc(row_step, 1)
                    dve.wait_ge(row_step, 8)
                    dve.tensor_tensor(row_c[0:4, :], row_b[0:4, :], row_m[0:4, :], ALU.subtract).then_inc(row_step, 1)
                    dve.tensor_copy(m_prev[:, 1:NB], row_m[0:4, P - 1:S - P:P]).then_inc(row_step, 1)
                if n == 12:
                    dve.wait_ge(row_step, 11)
                    c3 = row_c[0:4, :].rearrange("h (n t) -> h n t", n=NB)
                    a3 = row_all[0:4, :].rearrange("h (n t) -> h n t", n=NB)
                    dve.tensor_tensor(row_all[32:36, :].rearrange("h (n t) -> h n t", n=NB), c3,
                                      m_prev[:, :, None].broadcast_to([4, NB, P]), ALU.add).then_inc(row_step, 1)
                    dve.tensor_tensor(row_all[64:68, :].rearrange("h (n t) -> h n t", n=NB), a3,
                                      c3[:, :, P - 1:P].broadcast_to([4, NB, P]), ALU.add).then_inc(row_step, 1)

            def softmax_max(i, m):
                after(dve, scores_full, NB * i + m + 1)
                after(dve, neg_m_done, 2 * (NB * i + m))
                dve.nop().then_inc(scores_seen, 1)
                old = window(0) if m else neg_col[:, :, None].broadcast_to([P, 4, P])
                dve.copy_predicated(window(1), later[:, None, :].bitcast(mybir.dt.int16).broadcast_to([P, 4, P]), old).then_inc(window_merged, 1)
                after(dve, window_merged, NB * i + m + 1)
                dve.tensor_reduce(s_max[:, :], window(1), AX.X, ALU.max).then_inc(max_done, 1)
                after(dve, max_done, NB * i + m + 1)
                after(dve, exp_done, 5 * (NB * i + m))
                dve.scalar_tensor_tensor(out=neg_m[:, :], in0=s_max[:, :], scalar=-ATT_SCALE,
                                         in1=h_neg_sink[:, :, :].rearrange("p b a -> p (b a)"),
                                         op0=ALU.mult, op1=ALU.min).then_inc(neg_m_done, 1)
                after(dve, neg_m_done, 2 * (NB * i + m) + 1)
                dve.tensor_tensor(sink_d[:, :], neg_m[:, :], h_neg_sink[:, :, :].rearrange("p b a -> p (b a)"),
                                  ALU.subtract).then_inc(neg_m_done, 1)

            def rope(i, m):
                b = full("A", 6, i, m)
                if m == NB - 1:
                    free(dve, 0, 1, 2)
                qk = bank(b)[:, 0:5 * HD].rearrange("p (h d) -> p h d", d=32)
                tab = [P, 10, 32]
                after(dve, att_full, NB * i)
                dve.tensor_copy(v_tok[:, m, :], bank(b)[:, 5 * HD:6 * HD]).then_inc(v_copied, 1)
                dve.tensor_tensor(rot_c[:, :, :], qk, cos[:, m:m + 1, :].broadcast_to(tab), ALU.mult).then_inc(rope_product, 1)
                dve.tensor_tensor(rot_s[:, :, :], qk, sin[:, m:m + 1, :].broadcast_to(tab), ALU.mult).then_inc(rope_product, 1)
                after(dve, rope_product, 2 * (NB * i + m + 1))
                if m >= 2:
                    after(dve, qk_turned, NB * i + m - 1)
                r = roped[:, m % 2, :, :, :]
                pc = rot_c[:, :, :].rearrange("p (h a) d -> p h a d", a=2)
                ps = rot_s[:, :, :].rearrange("p (h a) d -> p h a d", a=2)
                dve.tensor_tensor(r[:, 0:5, 0, :], pc[:, :, 0, :], ps[:, :, 1, :], ALU.subtract).then_inc(bank_free[b], 1)
                dve.tensor_tensor(r[:, 0:5, 1, :], pc[:, :, 1, :], ps[:, :, 0, :], ALU.add).then_inc(rope_done, 1)
                after(dve, rope_done, 2 * (NB * i + m) + 1)
                after(dve, bank_free[b], unit("A", 6, i, m)[1] + 1)
                dve.tensor_copy(r[:, 5, :, :], r[:, 4, :, :]).then_inc(rope_done, 1)

            def q_low(i, m):
                after(dve, q_hi_ready, NB * i + m + 1)
                dve.tensor_tensor(q_parts[:, m % 2, :, 1, :], roped[:, m % 2, 0:4, :, :].rearrange("p h a d -> p h (a d)"),
                                  q_parts[:, m % 2, :, 0, :].bitcast(F32), ALU.subtract).then_inc(q_lo_ready, 1)

            def k_low(i, m):
                after(dve, qk_copied, 2 * (NB * i + m + 1))
                dve.tensor_tensor(k_lo[:, m * P:(m + 1) * P], bank(6)[:, 0:P], k_hi[:, m * P:(m + 1) * P].bitcast(F32),
                                  ALU.subtract).then_inc(k_lo_ready, 1)

            def normalise(i, m):
                after(dve, exp_done, 5 * (NB * i + m + 1))
                dve.tensor_tensor(p_den[:, :], p_sum[:, :], sink_e[:, :], ALU.add).then_inc(den_step, 1)
                after(dve, den_step, 2 * (NB * i + m) + 1)
                dve.reciprocal(p_rec[:, :], p_den[:, :]).then_inc(den_step, 1)
                after(dve, den_step, 2 * (NB * i + m) + 2)
                for g in range(4):
                    dve.tensor_scalar(prob[:, g, :], prob[:, g, :], p_rec[:, g:g + 1], None, ALU.mult).then_inc(probs_ready, 1)

            def split_window(i, m):
                after(dve, probs_turned, NB * i + m + 1)
                after(dve, att_full, NB * i + m)
                for part, keep in ((0, turned_old), (1, turned_new)):
                    if m or part:
                        dve.tensor_tensor(prob_t[:, part, :].rearrange("p (g t) -> p g t", g=4),
                                          bank(5).rearrange("p (g t) -> p g t", g=4),
                                          keep[:, None, :].broadcast_to([P, 4, P]), ALU.mult).then_inc(prob_t_ready, 1)

            def attend(i, before_head=None):
                src = neg_sink[:, bass.ds(4 * i, 4)].rearrange("p (a b) -> p b a", b=2)
                dve.tensor_scalar(h_neg_sink[:, :, :], src, 1.0, None, ALU.mult).then_inc(head_sinks, 1)
                after(dve, head_sinks, i + 1)
                for u in range(13):
                    if 4 <= u <= NB + 3:
                        softmax_max(i, u - 4)
                    if 3 <= u <= NB + 2:
                        k_low(i, u - 3)
                    if 5 <= u <= NB + 4:
                        split_window(i, u - 5)
                    if 2 <= u <= NB + 1:
                        q_low(i, u - 2)
                    if 4 <= u <= NB + 3:
                        normalise(i, u - 4)
                    if 1 <= u <= NB:
                        rope(i, u - 1)
                    if before_head is None:
                        gate_row_step(u)
                    elif u == 2:
                        gate_head(before_head)

            def gate_head(i):
                for e in (10, 11):
                    b, n = unit("A", 6, i, e)
                    after(dve, bank_free[b], n + 1)
                after(dve, att_copied, NB * (i + 1))
                for half in range(2):
                    t = slice(half * HALF, (half + 1) * HALF)
                    dst = y[:, bass.ds(2 * i, 2), t]
                    dve.tensor_tensor(dst, dst, silu_az[:, :, t], ALU.mult).then_inc(att_gated, 1)

            attend(0)
            with dve.Fori(0, KVH - 1, 1) as i:
                attend(i + 1, i)
            gate_head(KVH - 1)

            after(dve, att_gated, 2 * KVH)
            for half in range(2):
                t = slice(half * HALF, (half + 1) * HALF)
                for k in range(KT):
                    dve.wait_ge(y_hi_late if half else y_hi_ready, k + 1)
                    dve.tensor_tensor(y_lo[:, k, t], y[:, k, t], y_hi[:, k, t].bitcast(F32), ALU.subtract).then_inc(y_lo_ready, 1)
            dve.wait_ge(rows_turned, 1)
            for n in range(2):
                src = bank(2 + n).rearrange("p (n q h) -> p n q h", n=4, q=4)[:, :, :, 0:4].rearrange("p n q h -> p q h n")
                for q in range(4):
                    ins = dve.tensor_copy(cols[:, :, 4 * n:4 * n + 4, q], src[:, q, :, :])
                ins.then_inc(cols_step, 1)
            dve.wait_ge(cols_step, 2)
            dve.tensor_scalar(cols[:, :, :, 2], cols[:, :, :, 2], K_SCALE, None, ALU.mult).then_inc(cols_step, 1)
            with dve.Fori(0, 4, 1) as i:
                for k in range(2):
                    for half in range(2):
                        b0, n0 = unit("B", 4, i, 4 * k + half)
                        after(dve, bank_free[b0], n0 + 1)
                        if half == 0:
                            dve.wait_ge(mix_stored[k], 16 * (i + 1))
                        b = full("B", 4, i, 4 * k + 2 + half)
                        if half:
                            free(dve, 2 * k + 1)
                        after(dve, mix_ready, 4 * i + 2 * k + half)
                        dve.tensor_tensor(mix_a[:, k, half * HALF:(half + 1) * HALF], sig_a[:, half, :], bank(b),
                                          ALU.mult).then_inc(mix_ready, 1)
                        after(dve, mix_ready, 4 * i + 2 * k + half + 1)
                        dve.nop().then_inc(bank_free[b], 1)

            for b in range(2):
                dve.wait_ge(mix_stored[b], 16 * 5)
            dve.wait_ge(cols_step, 3)
            dve.memset(v_aug[:, :, MD:MV], 1.0).then_inc(cols_step, 1)

            def decay_scores(i, n):
                after(dve, s_full, NB * i + n + 1)
                after(dve, dec_ready, NB * i + n + 1)
                if n >= 2:
                    after(dve, intra_full, NB * i + n - 1)
                dve.scalar_tensor_tensor(out=s_dec[:, n % 2, :], in0=bank(3)[:, 0:P], scalar=K_SCALE,
                                         in1=dec[:, n * P:(n + 1) * P], op0=ALU.mult, op1=ALU.mult).then_inc(s_decayed, 1)

            def numerator(i, n):
                after(dve, intra_full, NB * i + n + 1)
                if n == 0:
                    dve.tensor_copy(num[:, 0, :], bank(5)[:, 0:MV]).then_inc(num_ready, 1)
                else:
                    after(dve, inter_ready, 7 * i + n)
                    dve.tensor_tensor(num[:, n, :], inter[:, :], bank(5)[:, 0:MV], ALU.add).then_inc(num_ready, 1)
                if n < NB - 1:
                    after(dve, kv_full, 7 * i + n + 1)
                    for f in range(2):
                        if n == 0:
                            dve.tensor_copy(state[:, f, :], bank(6 + f)[:, 0:MV]).then_inc(state_ready, 1)
                        else:
                            after(dve, state_ready, 14 * i + 2 * n + f)
                            dve.scalar_tensor_tensor(out=state[:, f, :], in0=state[:, f, :], scalar=dec[:, S + n:S + n + 1],
                                                     in1=bank(6 + f)[:, 0:MV], op0=ALU.mult, op1=ALU.add).then_inc(state_ready, 1)
                after(dve, num_ready, NB * i + n + 1)
                dve.tensor_tensor(h_den[:, n:n + 1], num[:, n, MD:MV], h_cols[:, n, 3:4], ALU.max).then_inc(h_den_done, 1)
                after(dve, h_den_done, 2 * (NB * i + n) + 1)
                dve.scalar_tensor_tensor(out=h_den[:, n:n + 1], in0=num[:, n, MD:MV], scalar=-1.0, in1=h_den[:, n:n + 1],
                                         op0=ALU.mult, op1=ALU.max).then_inc(h_den_done, 1)
                after(dve, h_den_done, 2 * (NB * i + n + 1))
                dve.reciprocal(h_rec[:, n:n + 1], h_den[:, n:n + 1]).then_inc(h_rec_done, 1)

            with dve.Fori(0, MH, 1) as i:
                after(dve, dec_ready, NB * i)
                after(dve, h_squared, NB * i)
                after(dve, k_weighted, NB * i)
                after(dve, h_turned, 4 * i)
                dve.tensor_scalar(h_cols[:, :, :], cols[:, bass.ds(i, 1), :, :].rearrange("p h n q -> p (h n) q"), 1.0, None, ALU.mult)
                for taps, row in ((taps_q, V_CQ), (taps_k, V_CK)):
                    for j in range(CW):
                        dve.tensor_scalar(taps[:, j, :], vecs[:, bass.ds(row + KT * j + 2 * i, 2)], 1.0, None, ALU.mult)
                dve.tensor_scalar(m_norm[:, :], vecs[:, bass.ds(V_MN + 2 * i, 2)], 1.0, None, ALU.mult)
                dve.memset(xpad[:, 0:CW - 1], 0.0).then_inc(head_set, 1)
                after(dve, head_set, i + 1)
                for e, (kind, n) in enumerate(C_UNITS):
                    b, uses = unit("C", 12, i, e)
                    if kind in ("mq", "mk") and n % 2:
                        f = n // 2 + (2 if kind == "mk" else 0)
                        taps = taps_k if kind == "mk" else taps_q
                        after(dve, bank_free[0], unit("C", 12, i, e - 1)[1] + 1 if b == 1 else uses + 1)
                        after(dve, bank_free[1], uses + 1 if b == 1 else unit("C", 12, i, e - 1)[1] + 1)
                        after(dve, conv_silu, 4 * i + f)
                        for j in range(CW):
                            if j == 0:
                                dve.tensor_scalar(conv[:, :], xpad[:, 0:S], taps[:, 0, n // 2:n // 2 + 1], None, ALU.mult).then_inc(conv_step, 1)
                            else:
                                after(dve, conv_step, 4 * (4 * i + f) + j)
                                dve.scalar_tensor_tensor(out=conv[:, :], in0=xpad[:, j:j + S], scalar=taps[:, j, n // 2:n // 2 + 1],
                                                         in1=conv[:, :], op0=ALU.mult, op1=ALU.add).then_inc(conv_step, 1)
                    if kind == "mv":
                        decay_scores(i, n)
                        if n >= 1:
                            numerator(i, n - 1)
                    if (kind, n) == ("mo", 0):
                        numerator(i, NB - 1)
                        after(dve, h_squared, NB * (i + 1))
                        dve.tensor_scalar(h_ms[:, :], h_ssq[:, :], 1.0 / MD, EPS, ALU.mult, ALU.add).then_inc(h_norm_step, 1)
                        after(dve, h_rms_done, i + 1)
                        dve.reciprocal(h_inv[:, :], h_rms[:, :]).then_inc(h_norm_step, 1)
                        after(dve, h_norm_step, 3 * i + 2)
                        dve.tensor_tensor(h_scale[:, :], h_inv[:, :], h_rec[:, :], ALU.mult).then_inc(h_norm_step, 1)
                        after(dve, h_norm_step, 3 * i + 3)
                        for m in range(NB):
                            dve.tensor_scalar(num[:, m, 0:MD], num[:, m, 0:MD], h_scale[:, m:m + 1], None, ALU.mult).then_inc(h_normed, 1)
                    if kind == "mo":
                        after(dve, bank_free[b], uses + 1)
                        g = gate_m[:, n // 2, (n % 2) * HALF:(n % 2 + 1) * HALF]
                        dve.scalar_tensor_tensor(out=g, in0=g, scalar=m_norm[:, n // 2:n // 2 + 1], in1=sig_o[:, :],
                                                 op0=ALU.mult, op1=ALU.mult).then_inc(gate_m_done, 1)
                for q in range(4):
                    f, half = q // 2, q % 2
                    after(dve, h_turned, 4 * i + q + 1)
                    after(dve, gate_m_done, 4 * (i + 1))
                    dst = y[:, bass.ds(2 * i + f, 1), half * HALF:(half + 1) * HALF]
                    dve.tensor_tensor(dst, bank(2 + q)[:, None, :], gate_m[:, f:f + 1, half * HALF:(half + 1) * HALF], ALU.mult).then_inc(ym_ready, 1)

            after(dve, ym_ready, 4 * MH)
            dve.memset(gate_acc[:, :], 0.0).then_inc(cols_step, 1)
            dve.wait_ge(cols_step, 5)
            with dve.Fori(0, 2, 1) as i:
                for s in range(4):
                    dve.wait_ge(w_gate_loaded[s % 2], 16 * (2 * i + s // 2 + 1))
                    after(dve, gate_sum, 4 * i + s)
                    dve.scalar_tensor_tensor(out=gate_acc[:, :], in0=w_gate[:, s % 2, :], scalar=silu_c[:, bass.ds(4 * i + s, 1)],
                                             in1=gate_acc[:, :], op0=ALU.mult, op1=ALU.add).then_inc(gate_sum, 1)
            dve.wait_ge(gate_row_loaded, 16)
            after(dve, gate_sum, KT)
            dve.tensor_tensor(gate_acc[0:1, :], gate_acc[0:1, :], gate_row[0:1, :], ALU.add).then_inc(gate_bias_added, 1)
            for half in range(2):
                t = slice(half * HALF, (half + 1) * HALF)
                for k in range(KT):
                    dve.wait_ge(y2_hi_ready, half * KT + k + 1)
                    dve.tensor_tensor(y_lo[:, k, t], y[:, k, t], y2_hi[:, k, t].bitcast(F32), ALU.subtract).then_inc(y2_lo_ready, 1)
            with dve.Fori(0, 2, 1) as i:
                for s in range(4):
                    for half in range(2):
                        n = 8 * i + 2 * s + half
                        t = slice(half * HALF, (half + 1) * HALF)
                        b = full("D2", 4, i, 2 * s + half)
                        if half:
                            free(dve, D_SLOTS[s])
                        after(dve, g_lo_ready, n)
                        dve.tensor_tensor(merged[:, None, :], sig_m[:, bass.ds(4 * i + s, 1), t], bank(b)[:, None, :], ALU.mult).then_inc(bank_free[b], 1)
                        dve.wait_ge(mix_loaded[s % 2], 16 * (2 * i + s // 2 + 1))
                        after(dve, bank_free[b], unit("D2", 4, i, 2 * s + half)[1] + 1)
                        dve.tensor_tensor(merged[:, :], merged[:, :], mix_in[:, s % 2, t], ALU.add).then_inc(merged_ready, 1)
                        after(dve, g_hi_ready, n + 1)
                        dve.tensor_tensor(g_lo[:, bass.ds(4 * i + s, 1), t], merged[:, None, :],
                                          g_hi[:, bass.ds(4 * i + s, 1), t].bitcast(F32), ALU.subtract).then_inc(g_lo_ready, 1)

            dve.wait_ge(gate_spread, 1)
            after(dve, merged_ready, 16)
            dve.tensor_copy(gate_b[:, :], pp[:, 6:8, :].rearrange("p b c -> p (b c)")).then_inc(gate_ready, 1)
            dve.wait_ge(gate_ready, 1)
            dve.wait_ge(fin_loaded, 16)
            for half in range(2):
                for n in range(NB):
                    e = half * NB + n
                    t = slice(half * HALF, (half + 1) * HALF)
                    b = full("E", 8, 0, e)
                    if e:
                        dve.wait_ge(res_added, e)
                    dve.tensor_tensor(gated[:, :], bank(b), gate_b[:, t], ALU.mult).then_inc(bank_free[b], 1)
                    dve.wait_ge(res_loaded[n], 16)
                    after(dve, bank_free[b], unit("E", 8, 0, e)[1] + 1)
                    dve.tensor_tensor(res[:, n, t], res[:, n, t], gated[:, :], ALU.add).then_inc(res_added, 1)
                    if half:
                        dve.wait_ge(res_squared, e + 1)
                        dve.tensor_tensor(o_sum[:, n:n + 1], o_ssq[:, n, 0:1], o_ssq[:, n, 1:2], ALU.add).then_inc(o_step, 1)
                        dve.wait_ge(o_step, 3 * n + 1)
                        dve.tensor_scalar(o_ms[:, n:n + 1], o_sum[:, n:n + 1], 1.0 / D, EPS, ALU.mult, ALU.add).then_inc(o_step, 1)
                        dve.wait_ge(o_rms_done, n + 1)
                        dve.reciprocal(o_rstd[:, n:n + 1], o_rms[:, n:n + 1]).then_inc(o_step, 1)
                        dve.wait_ge(o_step, 3 * n + 3)
                        for t in out_parts(n):
                            dve.scalar_tensor_tensor(out=res[:, n, t], in0=res[:, n, t], scalar=o_rstd[:, n:n + 1], in1=fin_w[:, t],
                                                     op0=ALU.mult, op1=ALU.mult).then_inc(out_ready, 1)


def kernel(x, c, positions, w_ada, b_ada, norm_w, w_in, b_if, att_sinks, conv_q, conv_k,
           m_norm_w, w_att_branch, w_m_branch, w_out, final_norm_w):
    import numpy as _np
    import concourse.bacc as _bacc
    from concourse import mybir as _mybir
    from concourse.bass_utils import run_bass_kernel_spmd as _run

    nc = _bacc.Bacc("TRN2", target_bir_lowering=False, num_devices=1)
    freqs = (_np.float32(10000.0) ** (-_np.arange(0, HD, 2, dtype=_np.float32) / _np.float32(HD))).astype(_np.float32)
    arrays = {
        "x": _np.ascontiguousarray(x).reshape(S, D),
        "c": _np.ascontiguousarray(c).reshape(D),
        "positions": _np.ascontiguousarray(positions).reshape(S),
        "w_ada": _np.ascontiguousarray(w_ada).reshape(D, 3 * D),
        "b_ada": _np.ascontiguousarray(b_ada).reshape(3 * D),
        "norm_w": _np.ascontiguousarray(norm_w).reshape(D),
        "w_in": _np.ascontiguousarray(w_in).reshape(D, GM + D),
        "b_if": _np.ascontiguousarray(b_if).reshape(2 * MH),
        "att_sinks": _np.ascontiguousarray(att_sinks).reshape(16),
        "conv_q": _np.ascontiguousarray(conv_q).reshape(CW * D),
        "conv_k": _np.ascontiguousarray(conv_k).reshape(CW * D),
        "m_norm_w": _np.ascontiguousarray(m_norm_w).reshape(D),
        "w_att": _np.ascontiguousarray(w_att_branch).reshape(D, D),
        "w_m": _np.ascontiguousarray(w_m_branch).reshape(D, D),
        "w_out": _np.ascontiguousarray(w_out).reshape(D, D),
        "final_norm_w": _np.ascontiguousarray(final_norm_w).reshape(D),
        "inv_freq": freqs,
    }
    aps = {n: nc.dram_tensor(n, a.shape, _mybir.dt.from_np(a.dtype), kind="ExternalInput").ap() for n, a in arrays.items()}
    f32 = _mybir.dt.float32
    out = nc.dram_tensor("out", (S, D), f32, kind="ExternalOutput").ap()
    row_pack = nc.dram_tensor("row_pack", (MH, S + NB), f32, kind="Internal").ap()
    merged_dram = nc.dram_tensor("merged_dram", (D, S), f32, kind="Internal").ap()
    build(nc, out=out, row_pack=row_pack, merged_dram=merged_dram, **aps)
    r = _run(nc, [arrays], core_ids=[0])
    return r.results[0]["out"].reshape(1, S, D)
```
